# Optimizing a Trainium2 kernel written in Bass

```python
import jax
import jax.numpy as jnp
from jax import lax
import numpy as np

D_MODEL = 1024
BATCH = 1
SEQ = 512
DEPTH = 2
DEC_BATCH = 8
DEC_SEQ = 4
PAST_LEN = 2048
PAGE_SIZE = 128

N_EVEN = (DEPTH + 1) // 2
N_ODD = DEPTH // 2
W_A = D_MODEL // 2
G_A = 8
DG_A = W_A // G_A
CHUNK = 128
W_B = D_MODEL // 2
H_B = 8
DH_B = W_B // H_B
Q_BLOCK = 128
SB_BIAS_INIT = -7.0
H_C = 4
DK_C = D_MODEL // H_C
DV_C = 2 * DK_C
RET_CHUNK = 128
ROPE_BASE = 10000.0
D_FF = ((8 * D_MODEL // 3 + 127) // 128) * 128
CONV_W = 3
ALPHA = (2 * DEPTH) ** 0.25
BETA = (8 * DEPTH) ** -0.25
LN_EPS = 1e-5

kernel_name = 'hybrid_gmlp_stickbreak_retention_step'

def _layer_norm(x, g, b):
    xf = x.astype(jnp.float32)
    mu = jnp.mean(xf, axis=-1, keepdims=True)
    var = jnp.mean(jnp.square(xf - mu), axis=-1, keepdims=True)
    y = (xf - mu) * lax.rsqrt(var + LN_EPS)
    return (y * g.astype(jnp.float32) + b.astype(jnp.float32)).astype(x.dtype)

def _rotary(x, pos):
    half = x.shape[-1] // 2
    inv = ROPE_BASE ** (-jnp.arange(half, dtype=jnp.float32) / half)
    ang = pos.astype(jnp.float32)[:, None] * inv[None, :]
    cos = jnp.cos(ang)[None, :, None, :]
    sin = jnp.sin(ang)[None, :, None, :]
    xf = x.astype(jnp.float32)
    x1, x2 = xf[..., :half], xf[..., half:]
    return jnp.concatenate([x1 * cos - x2 * sin, x1 * sin + x2 * cos], axis=-1).astype(x.dtype)

def _chunk_gmlp(u, v, w_s, b_s):
    B, T, G, dg = v.shape
    L = min(CHUNK, T)
    n = -(-T // L)
    pad = n * L - T
    w = jnp.tril(w_s[:, :L, :L])
    b = b_s[:, :L]
    vp = jnp.pad(v, ((0, 0), (0, pad), (0, 0), (0, 0))).reshape(B, n, L, G, dg)
    mixed = jnp.einsum('gts,bnsgd->bntgd', w, vp) + b.T[None, None, :, :, None]
    mixed = mixed.reshape(B, n * L, G, dg)[:, :T]
    return u * mixed

def _sb_weights(z, causal):
    log_keep = jnp.where(causal, -jax.nn.softplus(z), 0.0)
    shifted = jnp.concatenate([log_keep[..., 1:], jnp.zeros_like(log_keep[..., :1])], axis=-1)
    suffix = lax.cumsum(shifted, axis=3, reverse=True)
    return jnp.where(causal, jnp.exp(jax.nn.log_sigmoid(z) + suffix), 0.0)

def _sb_block(q, k, v, qpos, kpos, bias):
    scale = q.shape[-1] ** -0.5
    z = (jnp.einsum('bqhd,bkhd->bhqk', q.astype(jnp.float32), k.astype(jnp.float32)) * scale
         + bias.astype(jnp.float32)[None, :, None, None])
    a = _sb_weights(z, kpos[None, :] < qpos[:, None])
    return jnp.einsum('bhqk,bkhd->bqhd', a, v.astype(jnp.float32)).astype(q.dtype)

def _sb_self(q, k, v, bias):
    B, T, H, d = q.shape
    kpos = jnp.arange(T)
    if T <= Q_BLOCK:
        return _sb_block(q, k, v, kpos, kpos, bias)
    nb = T // Q_BLOCK
    qb = jnp.moveaxis(q.reshape(B, nb, Q_BLOCK, H, d), 1, 0)
    starts = jnp.arange(nb) * Q_BLOCK

    def one(args):
        qi, s = args
        return _sb_block(qi, k, v, s + jnp.arange(Q_BLOCK), kpos, bias)

    out = lax.map(one, (qb, starts))
    return jnp.moveaxis(out, 0, 1).reshape(B, T, H, d)

def _sb_decode(q, k, v, past_k, past_v, bias):
    P = past_k.shape[1]
    T = q.shape[1]
    scale = q.shape[-1] ** -0.5
    qf = q.astype(jnp.float32)
    z = (jnp.concatenate([
        jnp.einsum('bqhd,bkhd->bhqk', qf, past_k.astype(jnp.float32)),
        jnp.einsum('bqhd,bkhd->bhqk', qf, k.astype(jnp.float32))], axis=-1) * scale
         + bias.astype(jnp.float32)[None, :, None, None])
    qpos = P + jnp.arange(T)
    kpos = jnp.arange(P + T)
    a = _sb_weights(z, kpos[None, :] < qpos[:, None])
    out = (jnp.einsum('bhqk,bkhd->bqhd', a[..., :P], past_v.astype(jnp.float32))
           + jnp.einsum('bhqk,bkhd->bqhd', a[..., P:], v.astype(jnp.float32)))
    return out.astype(q.dtype)

def _ab_mixer(x, w_in, vln_g, vln_b, w_s, b_s, sb_bias, w_out, past_k, past_v):
    B, T, _ = x.shape
    h = x @ w_in
    u_a, v_a, q, k, v = jnp.split(h, [W_A, 2 * W_A, 2 * W_A + W_B, 2 * W_A + 2 * W_B], axis=-1)
    u_a = jax.nn.gelu(u_a).reshape(B, T, G_A, DG_A)
    v_a = _layer_norm(jax.nn.gelu(v_a), vln_g, vln_b).reshape(B, T, G_A, DG_A)
    a_out = _chunk_gmlp(u_a, v_a, w_s, b_s).reshape(B, T, W_A)
    q = q.reshape(B, T, H_B, DH_B)
    k = k.reshape(B, T, H_B, DH_B)
    v = v.reshape(B, T, H_B, DH_B)
    if past_k is None:
        b_out = _sb_self(q, k, v, sb_bias)
    else:
        b_out = _sb_decode(q, k, v, past_k, past_v, sb_bias)
    y = jnp.concatenate([a_out, b_out.reshape(B, T, W_B)], axis=-1) @ w_out
    return y, k, v, v_a

def _retention(q, k, v, s0):
    B, T, H, dk = q.shape
    dv = v.shape[-1]
    L = RET_CHUNK if T % RET_CHUNK == 0 else T
    n = T // L
    log_g = jnp.log1p(-jnp.power(2.0, -5.0 - jnp.arange(H, dtype=jnp.float32)))
    idx = jnp.arange(L, dtype=jnp.float32)
    diff = idx[:, None] - idx[None, :]
    causal = diff >= 0
    dmat = jnp.where(causal[None], jnp.exp(jnp.where(causal, diff, 0.0)[None] * log_g[:, None, None]), 0.0)
    q_dec = jnp.exp((idx[None, :] + 1.0) * log_g[:, None]).T[None, :, :, None]
    k_dec = jnp.exp((L - 1.0 - idx)[None, :] * log_g[:, None]).T[None, :, :, None]
    c_dec = jnp.exp(L * log_g)[None, :, None, None]

    def to_chunks(a):
        return jnp.moveaxis(a.astype(jnp.float32).reshape(B, n, L, H, a.shape[-1]), 1, 0)

    def step(S, inp):
        qc, kc, vc = inp
        sc = jnp.einsum('blhd,bmhd->bhlm', qc, kc) * dmat[None]
        o = jnp.einsum('bhlm,bmhe->blhe', sc, vc) + jnp.einsum('blhd,bhde->blhe', qc, S) * q_dec
        S = S * c_dec + jnp.einsum('bmhd,bmhe->bhde', kc * k_dec, vc)
        return S, o

    S, o = lax.scan(step, s0.astype(jnp.float32), (to_chunks(q), to_chunks(k), to_chunks(v)))
    o = jnp.moveaxis(o, 0, 1).reshape(B, T, H, dv)
    return o.astype(q.dtype), S

def _head_norm(o, g, b):
    B, T, H, dv = o.shape
    of = o.astype(jnp.float32)
    mu = jnp.mean(of, axis=-1, keepdims=True)
    var = jnp.mean(jnp.square(of - mu), axis=-1, keepdims=True)
    y = ((of - mu) * lax.rsqrt(var + LN_EPS)).reshape(B, T, H * dv)
    return (y * g.astype(jnp.float32) + b.astype(jnp.float32)).astype(o.dtype)

def _ret_mixer(x, w_in, gn_g, gn_b, w_out, s0, pos0):
    B, T, _ = x.shape
    h = x @ w_in
    q, k, v, g = jnp.split(h, [H_C * DK_C, 2 * H_C * DK_C, 2 * H_C * DK_C + H_C * DV_C], axis=-1)
    pos = pos0 + jnp.arange(T)
    q = _rotary(q.reshape(B, T, H_C, DK_C), pos)
    k = _rotary(k.reshape(B, T, H_C, DK_C), pos) * (DK_C ** -0.5)
    v = v.reshape(B, T, H_C, DV_C)
    o, S = _retention(q, k, v, s0)
    y = (jax.nn.silu(g) * _head_norm(o, gn_g, gn_b)) @ w_out
    return y, S

def _conv_ffn(x, w_up, conv_w, conv_b, w_down, conv_state):
    T = x.shape[1]
    h = x @ w_up
    g, val = jnp.split(h, 2, axis=-1)
    gp = jnp.concatenate([conv_state.astype(g.dtype), g], axis=1)
    c = conv_b
    for i in range(CONV_W):
        c = c + conv_w[i] * gp[:, i:i + T]
    y = (jax.nn.gelu(c) * val) @ w_down
    return y, gp[:, T:]

def setup_inputs(seed: int = 0) -> dict:
    key = jax.random.key(seed)
    ks = jax.random.split(key, 32)
    n_pages = PAST_LEN // PAGE_SIZE
    n_used = DEC_BATCH * n_pages
    n_phys = n_used + n_used // 4

    def nrm(k, shape, s):
        return jax.random.normal(k, shape, jnp.float32) * s

    d_mix = W_A + W_B
    d_ret_in = 2 * H_C * DK_C + 2 * H_C * DV_C
    page_table = jax.random.permutation(ks[6], n_phys)[:n_used].reshape(DEC_BATCH, n_pages).astype(jnp.int32)
    return {
        'x_prompt': nrm(ks[0], (BATCH, SEQ, D_MODEL), 1.0),
        'x_sample': nrm(ks[1], (DEC_BATCH, DEC_SEQ, D_MODEL), 1.0),
        'cache_sb_k': nrm(ks[2], (N_EVEN, n_phys, PAGE_SIZE, H_B, DH_B), 1.0),
        'cache_sb_v': nrm(ks[3], (N_EVEN, n_phys, PAGE_SIZE, H_B, DH_B), 1.0),
        'state_ret': nrm(ks[4], (N_ODD, DEC_BATCH, H_C, DK_C, DV_C), 0.5),
        'state_ffn_conv': nrm(ks[5], (DEPTH, DEC_BATCH, CONV_W - 1, D_FF), 1.0),
        'page_table': page_table,
        'w_in_ab': nrm(ks[7], (N_EVEN, D_MODEL, 2 * W_A + 3 * W_B), D_MODEL ** -0.5),
        'vln_g': 1.0 + nrm(ks[8], (N_EVEN, W_A), 0.02),
        'vln_b': nrm(ks[9], (N_EVEN, W_A), 0.02),
        'w_s': nrm(ks[10], (N_EVEN, G_A, CHUNK, CHUNK), CHUNK ** -0.5),
        'b_s': 1.0 + nrm(ks[11], (N_EVEN, G_A, CHUNK), 0.02),
        'sb_bias': SB_BIAS_INIT + nrm(ks[25], (N_EVEN, H_B), 0.1),
        'w_out_ab': nrm(ks[12], (N_EVEN, d_mix, D_MODEL), BETA * d_mix ** -0.5),
        'w_in_ret': nrm(ks[13], (N_ODD, D_MODEL, d_ret_in), D_MODEL ** -0.5),
        'gn_g': 1.0 + nrm(ks[14], (N_ODD, H_C * DV_C), 0.02),
        'gn_b': nrm(ks[15], (N_ODD, H_C * DV_C), 0.02),
        'w_out_ret': nrm(ks[16], (N_ODD, H_C * DV_C, D_MODEL), BETA * (H_C * DV_C) ** -0.5),
        'ln1_g': 1.0 + nrm(ks[17], (DEPTH, D_MODEL), 0.02),
        'ln1_b': nrm(ks[18], (DEPTH, D_MODEL), 0.02),
        'ln2_g': 1.0 + nrm(ks[19], (DEPTH, D_MODEL), 0.02),
        'ln2_b': nrm(ks[20], (DEPTH, D_MODEL), 0.02),
        'w_up': nrm(ks[21], (DEPTH, D_MODEL, 2 * D_FF), D_MODEL ** -0.5),
        'conv_w': nrm(ks[22], (DEPTH, CONV_W, D_FF), CONV_W ** -0.5),
        'conv_b': nrm(ks[23], (DEPTH, D_FF), 0.02),
        'w_down': nrm(ks[24], (DEPTH, D_FF, D_MODEL), BETA * D_FF ** -0.5),
    }

def reference(x_prompt, x_sample, cache_sb_k, cache_sb_v, state_ret, state_ffn_conv, page_table,
              w_in_ab, vln_g, vln_b, w_s, b_s, sb_bias, w_out_ab, w_in_ret, gn_g, gn_b, w_out_ret,
              ln1_g, ln1_b, ln2_g, ln2_b, w_up, conv_w, conv_b, w_down):
    dec_b, n_pages = page_table.shape
    past_len = n_pages * PAGE_SIZE
    xp, xs = x_prompt, x_sample
    bp, tp = xp.shape[0], xp.shape[1]
    sb_k_p, sb_v_p, sb_k_s, sb_v_s, chunk_v_s = [], [], [], [], []
    ret_p, ret_s, conv_p, conv_s = [], [], [], []
    for l in range(DEPTH):
        if l % 2 == 0:
            e = l // 2
            past_k = cache_sb_k[e][page_table].reshape(dec_b, past_len, H_B, DH_B)
            past_v = cache_sb_v[e][page_table].reshape(dec_b, past_len, H_B, DH_B)
            yp, kp, vp, _ = _ab_mixer(xp, w_in_ab[e], vln_g[e], vln_b[e], w_s[e], b_s[e], sb_bias[e], w_out_ab[e], None, None)
            ys, kn, vn, va = _ab_mixer(xs, w_in_ab[e], vln_g[e], vln_b[e], w_s[e], b_s[e], sb_bias[e], w_out_ab[e], past_k, past_v)
            sb_k_p.append(kp.reshape(bp, tp // PAGE_SIZE, PAGE_SIZE, H_B, DH_B))
            sb_v_p.append(vp.reshape(bp, tp // PAGE_SIZE, PAGE_SIZE, H_B, DH_B))
            sb_k_s.append(kn)
            sb_v_s.append(vn)
            chunk_v_s.append(va)
        else:
            o = l // 2
            s0 = jnp.zeros((bp, H_C, DK_C, DV_C), jnp.float32)
            yp, sp = _ret_mixer(xp, w_in_ret[o], gn_g[o], gn_b[o], w_out_ret[o], s0, 0)
            ys, ss = _ret_mixer(xs, w_in_ret[o], gn_g[o], gn_b[o], w_out_ret[o], state_ret[o], past_len)
            ret_p.append(sp)
            ret_s.append(ss)
        xp = _layer_norm(ALPHA * xp + yp, ln1_g[l], ln1_b[l])
        xs = _layer_norm(ALPHA * xs + ys, ln1_g[l], ln1_b[l])
        c0 = jnp.zeros((bp, CONV_W - 1, D_FF), xp.dtype)
        fp, cp = _conv_ffn(xp, w_up[l], conv_w[l], conv_b[l], w_down[l], c0)
        fs, cs = _conv_ffn(xs, w_up[l], conv_w[l], conv_b[l], w_down[l], state_ffn_conv[l])
        conv_p.append(cp)
        conv_s.append(cs)
        xp = _layer_norm(ALPHA * xp + fp, ln2_g[l], ln2_b[l])
        xs = _layer_norm(ALPHA * xs + fs, ln2_g[l], ln2_b[l])
    return (xp, xs, jnp.stack(sb_k_p), jnp.stack(sb_v_p), jnp.stack(sb_k_s), jnp.stack(sb_v_s),
            jnp.stack(chunk_v_s), jnp.stack(ret_p), jnp.stack(ret_s), jnp.stack(conv_p), jnp.stack(conv_s))


_drawn_inputs = setup_inputs


def setup_inputs(seed=0):
    import zlib

    import numpy as np

    out = dict(_drawn_inputs(seed))
    spreads = {}
    factors = {'cache_sb_k': 5.773,
     'cache_sb_v': 4.646,
     'vln_g': 25.588,
     'vln_b': 23.436,
     'b_s': 8.0,
     'sb_bias': 8.0,
     'gn_g': 69.908,
     'gn_b': 68.958,
     'conv_b': 8.0}
    for name, (base, spread) in spreads.items():
        noise = np.random.default_rng([zlib.crc32(name.encode()), seed]).standard_normal(out[name].shape)
        drawn = base * np.exp(spread * noise) if base else spread * noise
        out[name] = jnp.asarray(drawn.astype(out[name].dtype))
    for name, factor in factors.items():
        out[name] = (out[name] * factor).astype(out[name].dtype)
    return out
```

```python
from contextlib import ExitStack, contextmanager

import numpy as np

import concourse.bass as bass
from concourse import mybir

F32 = mybir.dt.float32
F32R = mybir.dt.float32r
I32 = mybir.dt.int32
ALU = mybir.AluOpType
ACT = mybir.ActivationFunctionType

P = 128
D = 1024
KD = D // P
TP, DEC_B, DEC_T = 512, 8, 4
TS = DEC_B * DEC_T
NT = TP + TS
HN = NT // 2
NB = TP // P
PAST = 2048
N_PAGES = PAST // P
LAYERS = 2
DFF = 2816
NFF = DFF // P
KF = NFF // 2
H_B, DH_B = 8, 64
H_C, DK, DV = 4, 256, 512
ALPHA = float((2 * LAYERS) ** 0.25)
EPS = 1e-5
MASKED = -1.0e30
GP = TP + 2 + DEC_B * (DEC_T + 2)
GC = GP - 2
CAUSAL = [TP - P * j for j in range(NB)]
ZOFF = [sum(CAUSAL[:j]) for j in range(NB)]
ZW = sum(CAUSAL)
SLOTS = 8
PER_SLOT = N_PAGES // SLOTS

N_IN_AB, N_OUT, N_UP, N_RIN = 20, KD, 2 * KF, 12
U_IN_AB = 0
U_OUT_AB = U_IN_AB + N_IN_AB
N_FFN = 2 * (N_UP + N_OUT)
N_RET = N_RIN + N_OUT
U_RET = U_OUT_AB + N_OUT + N_FFN
U_FFN = [U_OUT_AB + N_OUT, U_RET + H_C * N_RET]
U_ALL = U_FFN[1] + N_FFN

T_DEC = 0
T_KP = T_DEC + TP
T_KS = T_KP + NB
T_QD = T_KS + 1
T_SS = T_QD + TS
T_CD = T_SS + TS
T_GN = T_CD + 1
T_W = T_GN + 8
SO = 3
S0R = 4


class Count:

    def __init__(self, engine, sem):
        self.engine, self.sem, self.n, self.loops = engine, sem, 0, []

    def add(self, instruction):
        instruction.then_inc(self.sem, 1)
        self.n += 1

    def wait(self):
        value = self.n
        for reg, per in self.loops:
            value = reg * per + value
        self.engine.wait_ge(self.sem, value)

    @contextmanager
    def loop(self, reg, times, per):
        first = self.n
        self.loops.append((reg, per))
        yield
        self.loops.pop()
        assert self.n - first == per, f"{self.n - first} steps a turn, not {per}"
        self.n = first + per * times


def view(ap, *dims, off=0):
    return bass.AP(ap.tensor, ap.offset + off, [list(ap.ap[0])] + [list(d) for d in dims])


def halves(ap):
    return ap.rearrange("p (a n) -> p a n", a=2)


def build_program(nc, A):
    with ExitStack() as ctx:
        def sb(name, shape, dt=F32):
            return ctx.enter_context(nc.sbuf_tensor(name, shape, dt))

        def sem(name):
            return ctx.enter_context(nc.semaphore(name))

        x_hi = sb("x_hi", [P, KD, NT], F32R)
        x_lo = sb("x_lo", [P, KD, NT], F32R)
        y = sb("y", [P, KD, NT])
        w_raw = sb("w_raw", [P, 2, KF * P])
        w_hi = sb("w_hi", [P, 2, KF * P], F32R)
        w_lo = sb("w_lo", [P, 2, KF * P], F32R)
        cst = sb("cst", [P, 7, P])
        ident, ones, tri, mask_le, neg_ge, mean_mat = (cst[:, i, :] for i in range(6))
        negn = cst[0:TS, 6, 0:64]
        blockm = cst[0:TS, 6, 64:72]
        eps = cst[:, 6, 72:73]
        lnp = sb("lnp", [P, 4, 2, KD])
        cw = sb("cw", [P, LAYERS, NFF, 4])
        cstate = sb("cstate", [P, LAYERS, NFF, 2 * DEC_B])
        cso = sb("cso", [P, LAYERS, NFF, 2 + 2 * DEC_B])
        s1 = sb("s1", [P, NT])
        std = sb("std", [P, NT])
        sq = sb("sq", [P, 2, NT])
        ptab = sb("ptab", [1, DEC_B * N_PAGES], I32)
        B = ctx.enter_context(nc.psum_tensor("banks", [P, 8, 512], F32))

        def overlay(*tensors):
            with ExitStack() as s:
                return [s.enter_context(nc.sbuf_tensor(n, shape, *(dt or [F32]))) for n, shape, *dt in tensors]

        with ExitStack() as mixer0:
            uT, qT, kT, va_nat, v_nat, qbd, bias8, biasrow, spn, an, bsT, kv = [
                mixer0.enter_context(nc.sbuf_tensor(n, s, F32)) for n, s in (
                    ("uT", [P, 4, NT]), ("qT", [P, 4, NT]), ("kT", [P, 4, NT]),
                    ("va_nat", [P, NB + 1, 512]), ("v_nat", [P, NB + 1, 512]),
                    ("qbd", [P, 4, DEC_B, 8]), ("bias8", [P, H_B]), ("biasrow", [P, 32]),
                    ("spn", [P, 4, DEC_B, 8]), ("an", [TS, 4, DEC_B, 8]), ("bsT", [P, 4, TS]),
                    ("kv", [P, SLOTS, PER_SLOT, 512]))]
            wsT, w4, brep, vlng, vlnb, vst, vmv, vrs, gmix, zn, lnn = overlay(
                ("wsT", [P, 8, P]), ("w4", [TS, 8, TS]), ("brep", [P, 4, P]), ("vlng", [P, 512]),
                ("vlnb", [P, 512]), ("vst", [P, NB + 1, 6]), ("vmv", [P, NB + 1, 2]), ("vrs", [P, NB + 1]),
                ("gmix", [P, NT]), ("zn", [TS, 4, DEC_B, 8]), ("lnn", [TS, 4, DEC_B, 8]))
            zd, ld, sp17, inc17, smask, ad = overlay(
                ("zd", [P, 32, 16]), ("ld", [P, 32, 16]), ("sp17", [P, 32, 17]), ("inc17", [P, 32, 17]),
                ("smask", [P, 32, 17]), ("ad", [P, 32, 16]))
            zp, lp, tp1, tp0, qpair, kpair, vpair = overlay(
                ("zp", [P, ZW]), ("lp", [P, ZW]), ("tp1", [P, P]), ("tp0", [P, 2 * P]),
                ("qpair", [P, TP]), ("kpair", [P, TP]), ("vpair", [P, NB, P]))
        act_hi, act_lo, gp, gc, ge, af = overlay(
            ("act_hi", [P, KF, NT], F32R), ("act_lo", [P, KF, NT], F32R), ("gp", [P, GP]), ("gc", [P, GC]),
            ("ge", [P, GC]), ("af", [P, NT]))
        rqk, rvT, rg, rkn, rvn, scT, scs, tab, rope, onat, m_lo, s0, so, km, qm, rst, rmv, rrs = overlay(
            ("rqk", [P, 4, NT]), ("rvT", [P, 4, NT]), ("rg", [P, 4, NT]), ("rkn", [P, NB + 1, DK]),
            ("rvn", [P, NB + 1, DV]), ("scT", [P, ZW]), ("scs", [TS, TS]), ("tab", [P, T_W]),
            ("rope", [P, 2, NT]), ("onat", [P, NB + 1, DV]), ("m_lo", [P, 4, NT], F32R),
            ("s0", [P, S0R, 2, DV]), ("so", [P, SO, 2, DV]), ("km", [TS, 2, DK]), ("qm", [P, 2, DEC_B, TS]),
            ("rst", [P, NB + 1, 6]), ("rmv", [P, NB + 1, 2]), ("rrs", [P, NB + 1]))
        m_hi, = overlay(("m_hi", [P, 4, NT], F32R))
        ropet = onat[:, :, :].rearrange("p a n -> p (a n)")

        w_landed = [sem("w_landed_0"), sem("w_landed_1")]
        hi_ready, lo_ready, tile_done = sem("w_hi_ready"), sem("w_lo_ready"), sem("tile_done")
        evicted = [sem("tile_evicted_0"), sem("tile_evicted_1")]
        const_in, x_in, mix_in = sem("const_in"), sem("x_in"), sem("mixer_const_in")
        x_hi_ready, x_ready = sem("x_hi_ready"), sem("x_ready")
        d_step, a_step, g_step = sem("vector_step"), sem("scalar_step"), sem("pool_step")
        nat_a, nat_b, cop_a, cop_b = (sem(n) for n in ("va_transposed", "v_transposed", "va_copied", "v_copied"))
        va_var, va_std, va_ready, ws_ready = (sem(n) for n in ("va_var", "va_std", "va_normed", "ws_masked"))
        gm_mixed, gm_out, gm_hi, gm_lo = (sem(n) for n in ("gmlp_mixed", "gmlp_gated", "gmlp_hi", "gmlp_lo"))
        zeroed, qbd_ready = sem("zeroed"), sem("qbd_ready")
        zn_done, zn_ready, lnn_ready, spn_ready, rn_done, znr_ready, an_ready = (
            sem("new_" + n) for n in ("z_done", "z_ready", "log_ready", "sp_ready", "r_done", "zr_ready", "a_ready"))
        kv_landed = [sem(f"kv_landed_{s}") for s in range(SLOTS)]
        kv_used = sem("kv_slot_used")
        z_ready, log_ready, sp_ready, r_done, zr_ready, a_ready, o_taken = (
            sem("dec_" + n) for n in ("z_ready", "log_ready", "sp_ready", "r_done", "zr_ready", "a_ready", "o_taken"))
        bs_hi, bs_lo = sem("dec_out_hi"), sem("dec_out_lo")
        pk_ready, pqk_done, pz_ready, plog_ready, psp_ready, pr_done, pzr_ready, pa_ready, pav_done, po_hi, po_lo = (
            sem("pr_" + n) for n in ("kv_ready", "qk_done", "z_ready", "log_ready", "sp_ready", "r_done",
                                     "zr_ready", "a_ready", "av_done", "o_hi", "o_lo"))
        y_loaded, y_scaled = sem("residual_loaded"), sem("residual_scaled")
        s_sum, m_done, c_ready, sq_ready, sq_used, std_ready, rs_ready, aff_ready, lnhi_ready, ln_done = (
            sem("ln_" + n) for n in ("sum_ready", "mean_done", "centred", "square_ready", "square_used",
                                     "std_ready", "scaled", "affine_ready", "hi_ready", "lo_ready"))
        conv_done, gelu_ready, act_ready = sem("conv_done"), sem("gelu_ready"), sem("act_ready")
        roped, rt_done, rk_ready, rv_ready = sem("roped"), sem("ret_transposed"), sem("ret_k_ready"), sem("ret_v_ready")
        rv_done = sem("ret_v_transposed")
        qm_ready = sem("ret_q_decayed")
        sc_done, sc_ready, scs_done, scs_ready = (sem("ret_" + n) for n in (
            "scores_done", "scores_ready", "sample_scores_done", "sample_scores_ready"))
        st_done, so_ready = sem("state_done"), sem("state_out_ready")
        s0_landed = [sem(f"state_landed_{s}") for s in range(S0R)]
        so_stored = [sem(f"state_stored_{s}") for s in range(SO)]
        km_ready = sem("ret_k_masked")
        ro_done, ro_copied, rvar_ready, rstd_ready, rnorm = (sem("ret_" + n) for n in (
            "o_done", "o_copied", "var_ready", "std_ready", "o_normed"))
        rb_done, rg_taken, m_ready, mhi_ready, mlo_ready = (sem("ret_" + n) for n in (
            "o_back", "o_back_taken", "gated", "gated_hi", "gated_lo"))
        tab_in, rope_in = sem("ret_table_in"), sem("rope_in")
        stored = sem("stored")
        turns = sem("turns")

        block = ctx.enter_context(nc.Block())

        def bank_pair(j):
            return B[:, 2 * j:2 * j + 2, 0:HN]

        def apart(e):
            e.sem_inc(turns, 1)

        def stream(e, n, k, k_next, body):
            with e.Fori(0, n // 2 - 1) as i:
                for j in range(2):
                    body(i * 2 + j, j, k)
            for j in range(2):
                body(n - 2 + j, j, k_next)

        @block.sync
        def _(sp):
            def load(dram, local, u, j, k):
                sp.wait_ge(lo_ready, u - 1)
                sp.dma_start(w_raw[:, j, 0:k * P], dram[bass.ds(local, 1)].rearrange("o p k -> (o p) k"))\
                    .then_inc(w_landed[j], 16)

            def load_all(dram, first, base, n, k, skip=0):
                with sp.Fori(skip // 2, n // 2) as i:
                    for j in range(2):
                        load(dram, i * 2 + (first + j), i * 2 + (base + j), j, k)

            sp.dma_start(w_raw[:, 0, 0:KD * P], A["w_in_ab"][0]).then_inc(w_landed[0], 16)
            sp.dma_start(y[:, :, :], A["xT"]).then_inc(x_in, 16)
            sp.dma_start(w_raw[:, 1, 0:KD * P], A["w_in_ab"][1]).then_inc(w_landed[1], 16)
            sp.dma_start(cst[:, :, :], A["cst"]).then_inc(const_in, 16)
            sp.dma_start(ptab[:, :], A["ptab"]).then_inc(const_in, 16)
            for dst, name in ((lnp[:, :, :, :], "lnp"), (cw[:, :, :, :], "cw"), (cstate[:, :, :, :], "cstate")):
                sp.dma_start(dst, A[name]).then_inc(const_in, 16)
            for dst, name in ((wsT[:, :, :], "wsT"), (w4[:, :, :], "w4"), (brep[:, :, :], "brep"),
                              (vlng[:, :], "vlng"), (vlnb[:, :], "vlnb"), (bias8[:, :], "bias8")):
                sp.dma_start(dst, A[name]).then_inc(mix_in, 16)
            load_all(A["w_in_ab"], 0, U_IN_AB, N_IN_AB, KD, skip=2)
            load_all(A["w_out_ab"], 0, U_OUT_AB, 2, KD)
            sp.wait_ge(const_in, 5 * 16)

            def load_kv(cache, b, group):
                for s in range(SLOTS):
                    pages = [sp.value_load(ptab[0:1, bass.ds(b * N_PAGES + (PER_SLOT * s + g), 1)],
                                           min_val=0, max_val=A["kc"].shape[0] - 1) for g in range(PER_SLOT)]
                    if not isinstance(group, int) or group:
                        sp.wait_ge(kv_used, group * SLOTS + (s + 1 - SLOTS))
                    for g in range(PER_SLOT):
                        sp.dma_start(kv[:, s, g, :], cache[bass.ds(pages[g], 1)].rearrange("o p k -> (o p) k"))\
                            .then_inc(kv_landed[s], 16)

            load_kv(A["kc"], 0, 0)
            with sp.Fori(0, DEC_B - 1) as b:
                load_kv(A["kc"], b + 1, b * 2 + 1)
                load_kv(A["vc"], b, b * 2 + 2)
            load_kv(A["vc"], DEC_B - 1, 2 * DEC_B - 1)
            load_all(A["w_out_ab"], 0, U_OUT_AB, N_OUT, KD, skip=2)

            def load_ffn(l):
                for half in range(2):
                    base = U_FFN[l] + half * (N_UP + N_OUT)
                    load_all(A["w_up"], (2 * l + half) * N_UP, base, N_UP, KD)
                    load_all(A["w_dn"], (2 * l + half) * N_OUT, base + N_UP, N_OUT, KF)

            load_ffn(0)
            with sp.Fori(0, H_C) as h:
                base = h * N_RET + U_RET
                for i in range(N_RIN):
                    load(A["w_rin"], h * N_RIN + i, base + i, i % 2, KD)
                for i in range(2):
                    load(A["w_rout"], h * N_OUT + i, base + (N_RIN + i), i % 2, 4)
                sp.dma_start(tab[:, :], A["tab"][bass.ds(h, 1)].rearrange("o p k -> (o p) k")).then_inc(tab_in, 16)

                def load_state(b):
                    if b >= S0R:
                        sp.wait_ge(so_ready, h * (DEC_B + 1) + (b - S0R + 2))
                    sp.dma_start(s0[:, b % S0R, :, :].rearrange("p a n -> p (a n)"),
                                 A["s0"][bass.ds(h * DEC_B + b, 1)].rearrange("o p k -> (o p) k"))\
                        .then_inc(s0_landed[b % S0R], 16)

                def store_state(n):
                    sp.wait_ge(so_ready, h * (DEC_B + 1) + (n + 1))
                    dst = A["ret_p"][bass.ds(h, 1)] if n == 0 else A["ret_s"][bass.ds(h * DEC_B + (n - 1), 1)]
                    sp.dma_start(dst.rearrange("o p k -> (o p) k"),
                                 so[:, n % SO, :, :].rearrange("p a n -> p (a n)")).then_inc(so_stored[n % SO], 16)

                for b in range(S0R):
                    load_state(b)
                for n in range(DEC_B + 1):
                    store_state(n)
                    if n and n - 1 + S0R < DEC_B:
                        load_state(n - 1 + S0R)
                for i in range(2, N_OUT):
                    load(A["w_rout"], h * N_OUT + i, base + (N_RIN + i), i % 2, 4)
            load_ffn(1)
            sp.wait_ge(stored, 6 * 16)
            for n in range(SO):
                sp.wait_ge(so_stored[n], 16 * H_C * (DEC_B + 1) // SO + 16)

        @block.gpsimd
        def _(pool):
            step = Count(pool, g_step)
            nc.gpsimd.memset(qbd[:, :, :, :], 0.0).then_inc(zeroed, 1)
            nc.gpsimd.memset(spn[:, :, :, :], 0.0).then_inc(zeroed, 1)
            pool.wait_ge(evicted[1], N_IN_AB // 2 + 1)
            pool.wait_ge(evicted[0], N_IN_AB // 2 + 1)
            pool.dma_start(A["kT"], kT[:, :, :]).then_inc(stored, 16)
            pool.dma_start(A["vT"], y[:, 4:8, :]).then_inc(stored, 16)
            pool.wait_ge(nat_a, NB + 1)
            pool.wait_ge(nat_b, NB + 1)
            pool.wait_ge(stored, 2 * 16)
            pool.dma_start(y[:, :, :], A["xT"]).then_inc(y_loaded, 16)
            pool.wait_ge(y_loaded, 16)
            nc.gpsimd.tensor_scalar(y[:, :, :], y[:, :, :], ALPHA, None, ALU.mult).then_inc(y_scaled, 1)
            pool.wait_ge(va_ready, NB + 1)
            pool.dma_start(A["chunk_v"], va_nat[0:TS, NB, :]).then_inc(stored, 16)

            def scale_residual(n):
                for m in range(KD):
                    pool.wait_ge(ln_done, n * KD + m + 1)
                    nc.gpsimd.tensor_scalar(y[:, m, :], y[:, m, :], ALPHA, None, ALU.mult).then_inc(y_scaled, 1)

            scale_residual(0)
            pool.wait_ge(y_scaled, 1 + KD)
            scale_residual(1)
            pool.wait_ge(y_scaled, 1 + 2 * KD)
            pool.dma_start(rope[:, :, :], A["rope"]).then_inc(rope_in, 16)
            nc.gpsimd.memset(qm[:, :, :, :], 0.0).then_inc(zeroed, 1)
            pool.wait_ge(rope_in, 16)
            with pool.Fori(0, H_C) as h, step.loop(h, H_C, 8):
                for qk in range(2):
                    for j in range(2):
                        pool.wait_ge(evicted[j], h * (N_RET // 2) + (U_RET // 2 + qk + 2))
                    x1, x2 = rqk[:, 2 * qk, :], rqk[:, 2 * qk + 1, :]
                    t = [ropet[:, n * NT:(n + 1) * NT] for n in range(4)]
                    for n, (a, c) in enumerate(((x1, 0), (x2, 1), (x2, 0), (x1, 1))):
                        step.add(nc.gpsimd.tensor_tensor(t[n], a, rope[:, c, :], ALU.mult))
                    step.wait()
                    nc.gpsimd.tensor_tensor(x1, t[0], t[1], ALU.subtract).then_inc(roped, 1)
                    nc.gpsimd.tensor_tensor(x2, t[2], t[3], ALU.add).then_inc(roped, 1)
                    pool.wait_ge(roped, h * 4 + (2 * qk + 2))
            scale_residual(2)
            pool.wait_ge(ln_done, 4 * KD)
            for l in range(LAYERS):
                pool.dma_start(A["conv_out"][l], cso[:, l, :, :].rearrange("p a n -> p (a n)")).then_inc(stored, 16)
            pool.dma_start(A["yT"], y[:, :, :]).then_inc(stored, 16)

        @block.scalar
        def _(act):
            step = Count(act, a_step)

            def copy(out, in_):
                return nc.scalar.activation(out, in_, ACT.Copy)

            def split(u, j, k):
                act.wait_ge(w_landed[j], (u - j) * 8 + 16)
                act.wait_ge(tile_done, u - 1)
                copy(w_hi[:, j, 0:k * P], w_raw[:, j, 0:k * P]).then_inc(hi_ready, 1)

            def first_split(j):
                act.wait_ge(w_landed[j], 16)
                copy(w_hi[:, j, 0:KD * P], w_raw[:, j, 0:KD * P]).then_inc(hi_ready, 1)

            first_split(0)
            act.wait_ge(x_in, 16)
            for m in range(KD):
                copy(x_hi[:, m, :], y[:, m, :]).then_inc(x_hi_ready, 1)
            first_split(1)
            act.wait_ge(x_ready, 1)
            act.wait_ge(x_hi_ready, KD)

            def evict_ab(base, dst, d0, func):
                with act.Fori(0, 2) as i:
                    for j in range(2):
                        split(i * 2 + (base + j + 2), j, KD)
                        nc.scalar.activation(halves(view(dst[:, 0, :], (1, NT), off=(i * 2 + (d0 + j)) * NT)),
                                             bank_pair(j), func).then_inc(evicted[j], 1)

            evict_ab(0, y, 0, ACT.Gelu_apprx_tanh)
            evict_ab(4, y, 4, ACT.Copy)
            evict_ab(8, uT, 0, ACT.Gelu_apprx_tanh)
            evict_ab(12, qT, 0, ACT.Copy)
            evict_ab(16, kT, 0, ACT.Copy)

            for t in range(NB + 1):
                rows = P if t < NB else TS
                act.wait_ge(nat_a, t + 1)
                copy(va_nat[0:rows, t, :], B[0:rows, 4 + t % 2, :]).then_inc(cop_a, 1)
            act.wait_ge(const_in, 5 * 16)
            act.wait_ge(va_var, 1)
            nc.scalar.activation(vrs[:, :], vmv[:, :, 1], ACT.Sqrt, bias=eps).then_inc(va_std, 1)
            for pr in range(4):
                act.wait_ge(gm_out, pr + 1)
                copy(x_hi[:, pr, :], uT[:, pr, :]).then_inc(gm_hi, 1)

            def log_part(z, l, ready, n, done):
                act.wait_ge(ready, n)
                step.add(nc.scalar.activation(l, z, ACT.Abs))
                step.wait()
                step.add(nc.scalar.activation(l, l, ACT.Exp, scale=-1.0))
                step.wait()
                nc.scalar.activation(l, l, ACT.Ln, bias=1.0).then_inc(done, 1)

            flat = "p a b c -> p (a b c)"
            log_part(zn[:, :, :, :].rearrange(flat), lnn[:, :, :, :].rearrange(flat), zn_ready, 1, lnn_ready)
            act.wait_ge(znr_ready, 1)
            nc.scalar.activation(an[:, :, :, :], zn[:, :, :, :], ACT.Exp).then_inc(an_ready, 1)

            zf, lf, af_ = (t[:, :, :].rearrange("p a b -> p (a b)") for t in (zd, ld, ad))
            log_part(zf, lf, z_ready, 1, log_ready)
            with act.Fori(0, DEC_B - 1) as b, step.loop(b, DEC_B - 1, 2):
                act.wait_ge(zr_ready, b + 2)
                nc.scalar.activation(af_, af_, ACT.Exp).then_inc(a_ready, 1)
                log_part(zf, lf, z_ready, b + 2, log_ready)
            act.wait_ge(zr_ready, DEC_B + 1)
            nc.scalar.activation(af_, af_, ACT.Exp).then_inc(a_ready, 1)
            act.wait_ge(o_taken, 2 * DEC_B + 2)
            copy(x_hi[:, 4:8, TP:NT], bsT[:, :, :]).then_inc(bs_hi, 1)

            with act.Fori(0, 4) as c, step.loop(c, 4, 4):
                for h2 in range(2):
                    log_part(zp[:, :], lp[:, :], pz_ready, c * 2 + (h2 + 2), plog_ready)
                    act.wait_ge(pzr_ready, c * 2 + (h2 + 2))
                    nc.scalar.activation(zp[:, :], zp[:, :], ACT.Exp).then_inc(pa_ready, 1)

            def splits(base, n, k, k_next):
                stream(act, n, k, k_next, lambda i, j, kk: split(i + (base + 2), j, kk))

            def norm(n):
                for m in range(KD):
                    act.wait_ge(c_ready, n * KD + m + 1)
                    if m >= 2:
                        act.wait_ge(sq_used, n * KD + m - 1)
                    nc.scalar.activation(sq[:, m % 2, :], y[:, m, :], ACT.Square).then_inc(sq_ready, 1)
                act.wait_ge(sq_used, n * KD + KD)
                nc.scalar.activation(halves(std[:, :]), B[:, 6:8, 0:HN], ACT.Sqrt, bias=eps).then_inc(std_ready, 1)
                for m in range(KD):
                    act.wait_ge(rs_ready, n * (KD + 1) + m + 2)
                    nc.scalar.activation(y[:, m, :], y[:, m, :], ACT.Identity, scale=lnp[:, n, 0, m:m + 1],
                                         bias=lnp[:, n, 1, m:m + 1]).then_inc(aff_ready, 1)
                    act.wait_ge(aff_ready, n * KD + m + 1)
                    copy(x_hi[:, m, :], y[:, m, :]).then_inc(lnhi_ready, 1)

            def ffn(l, k_last):
                for half in range(2):
                    base = U_FFN[l] + half * (N_UP + N_OUT)
                    pairs = (2 * l + half) * KF

                    def pair(i, k):
                        split(i * 2 + (base + 2), 0, k)
                        act.wait_ge(conv_done, i + (pairs + 1))
                        step.add(copy(gp[:, 2:2 + HN], B[:, 0, 0:HN]))
                        step.add(copy(gp[:, 2 + HN:2 + TP], B[:, 1, 0:TP - HN]))
                        copy(view(gp[:, 0:1], (6, DEC_B), (1, DEC_T), off=TP + 4),
                             B[:, 1, TP - HN:HN].rearrange("p (b t) -> p b t", t=DEC_T)).then_inc(evicted[0], 1)
                        split(i * 2 + (base + 3), 1, k)
                        act.wait_ge(conv_done, i + (pairs + 2))
                        nc.scalar.activation(ge[:, :], gc[:, :], ACT.Gelu_apprx_tanh).then_inc(gelu_ready, 1)

                    with act.Fori(0, KF - 1) as i, step.loop(i, KF - 1, 2):
                        pair(i, KD)
                    pair(KF - 1, KF)
                    k_next = KD if half == 0 else k_last
                    if k_next:
                        splits(base + N_UP, N_OUT, KF, k_next)
                    else:
                        with act.Fori(0, N_OUT // 2 - 1) as i:
                            for j in range(2):
                                split(i * 2 + (base + N_UP + 2 + j), j, KF)

            splits(U_OUT_AB, N_OUT, KD, KD)
            norm(0)
            ffn(0, KD)
            norm(1)
            with act.Fori(0, H_C) as h, step.loop(h, H_C, 0):
                base = h * N_RET + U_RET
                for i in range(N_RIN):
                    split(base + (i + 2), i % 2, KD if i < N_RIN - 2 else 4)
                    dst = rqk[:, i, :] if i < 4 else rvT[:, i - 4, :] if i < 8 else rg[:, i - 8, :]
                    nc.scalar.activation(halves(dst), bank_pair(i % 2), ACT.Copy if i < 8 else ACT.Silu)\
                        .then_inc(evicted[i % 2], 1)
                for t in range(NB + 1):
                    rows = P if t < NB else TS
                    act.wait_ge(rv_done, h * (NB + 1) + (t + 1))
                    copy(rvn[0:rows, t, :], B[0:rows, 6 + t % 2, :]).then_inc(rv_ready, 1)
                for t, bank in enumerate((3, 0, 1, 2, 6)):
                    rows = P if t else TS
                    act.wait_ge(ro_done, h * (NB + 1) + (t + 1))
                    copy(onat[0:rows, (t - 1) % (NB + 1), :], B[0:rows, bank, :]).then_inc(ro_copied, 1)
                act.wait_ge(rvar_ready, h + 1)
                nc.scalar.activation(rrs[:, :], rmv[:, :, 1], ACT.Sqrt, bias=eps).then_inc(rstd_ready, 1)
                for et in range(4):
                    act.wait_ge(m_ready, h * 4 + (et + 1))
                    copy(m_hi[:, et, :], rvT[:, et, :]).then_inc(mhi_ready, 1)
                for i in range(N_OUT):
                    split(base + (N_RIN + i + 2), i % 2, 4 if i < N_OUT - 2 else KD)
            norm(2)
            ffn(1, None)
            norm(3)

        @block.vector
        def _(dve):
            step = Count(dve, d_step)
            V = nc.vector

            def low(u, j, k):
                dve.wait_ge(hi_ready, u + 1)
                V.tensor_tensor(w_lo[:, j, 0:k * P], w_raw[:, j, 0:k * P], w_hi[:, j, 0:k * P].bitcast(F32),
                                ALU.subtract).then_inc(lo_ready, 1)

            for first, value in ((evicted[0], 1), (evicted[1], 1), (conv_done, 1), (zr_ready, 1), (o_taken, 2),
                                 (pav_done, 1), (pz_ready, 1), (pzr_ready, 1), (po_lo, 1),
                                 *((s, 16) for s in so_stored)):
                dve.sem_inc(first, value)
            low(0, 0, KD)
            for m in range(KD):
                dve.wait_ge(x_hi_ready, m + 1)
                last = V.tensor_tensor(x_lo[:, m, :], y[:, m, :], x_hi[:, m, :].bitcast(F32), ALU.subtract)
                if m < KD - 1:
                    step.add(last)
            last.then_inc(x_ready, 1)
            low(1, 1, KD)
            with dve.Fori(0, N_IN_AB // 2) as i:
                for j in range(2):
                    low(i * 2 + (2 + j), j, KD)

            dve.wait_ge(const_in, 5 * 16)
            dve.wait_ge(mix_in, 6 * 16)
            for g in range(8):
                step.add(V.tensor_tensor(wsT[:, g, :], wsT[:, g, :], mask_le, ALU.mult))
            step.add(V.tensor_copy(biasrow[:, :].rearrange("p (h q) -> p h q", q=4),
                                   view(bias8[:, :], (1, H_B), (0, 4))))
            step.add(V.memset(vmv[:, :, :], 1.0))
            w4m = cst[0:TS, 6, 80:80 + TS]
            V.tensor_tensor(w4[:, :, :], w4[:, :, :], view(w4m, (0, 8), (1, TS)), ALU.mult).then_inc(ws_ready, 1)
            for t in range(NB + 1):
                rows = P if t < NB else TS
                dve.wait_ge(nat_b, t + 1)
                V.tensor_copy(v_nat[0:rows, t, :], B[0:rows, 6 + t % 2, :]).then_inc(cop_b, 1)
                dve.wait_ge(cop_a, t + 1)
                step.add(V.bn_stats(vst[0:rows, t, :], va_nat[0:rows, t, :]))
            step.wait()
            for t in range(NB + 1):
                rows = P if t < NB else TS
                last = V.bn_aggr(vmv[0:rows, t, :], vst[0:rows, t, :])
                if t < NB:
                    step.add(last)
            last.then_inc(va_var, 1)
            dve.wait_ge(va_std, 1)
            step.add(V.reciprocal(vrs[:, :], vrs[:, :]))
            step.wait()
            dve.wait_ge(va_var, 1)
            for t in range(NB + 1):
                rows = P if t < NB else TS
                step.add(V.tensor_scalar(va_nat[0:rows, t, :], va_nat[0:rows, t, :], vmv[0:rows, t, 0:1],
                                         vrs[0:rows, t:t + 1], ALU.subtract, ALU.mult))
            step.wait()
            for t in range(NB + 1):
                rows = P if t < NB else TS
                step.add(V.tensor_tensor(va_nat[0:rows, t, :], va_nat[0:rows, t, :], vlng[0:rows, :], ALU.mult))
            step.wait()
            for t in range(NB + 1):
                rows = P if t < NB else TS
                V.tensor_tensor(va_nat[0:rows, t, :], va_nat[0:rows, t, :], vlnb[0:rows, :], ALU.add)\
                    .then_inc(va_ready, 1)

            dve.wait_ge(zeroed, 2)
            for h2 in range(2):
                rows = slice(64 * h2, 64 * h2 + 64)
                V.tensor_copy(qbd[rows, :, :, 4 * h2:4 * h2 + 4],
                              qT[rows, :, TP:NT].rearrange("p c (b t) -> p c b t", t=DEC_T)).then_inc(qbd_ready, 1)

            for pr in range(4):
                dve.wait_ge(gm_mixed, pr + 2)
                if pr:
                    dve.wait_ge(gm_out, pr)
                step.add(V.tensor_tensor(gmix[:, 0:TP].rearrange("p (n t) -> p n t", t=P),
                                         B[:, pr, :].rearrange("p (n t) -> p n t", t=P),
                                         view(brep[:, pr, :], (0, NB), (1, P)), ALU.add))
                step.add(V.tensor_tensor(gmix[:, TP:NT].rearrange("p (b t) -> p b t", t=DEC_T),
                                         B[:, 4, pr * TS:(pr + 1) * TS].rearrange("p (b t) -> p b t", t=DEC_T),
                                         view(brep[:, pr, :], (0, DEC_B), (1, DEC_T)), ALU.add))
                step.wait()
                V.tensor_tensor(uT[:, pr, :], gmix[:, :], uT[:, pr, :], ALU.mult).then_inc(gm_out, 1)
            for pr in range(4):
                dve.wait_ge(gm_hi, pr + 1)
                V.tensor_tensor(x_lo[:, pr, :], uT[:, pr, :], x_hi[:, pr, :].bitcast(F32), ALU.subtract)\
                    .then_inc(gm_lo, 1)

            dve.wait_ge(zn_done, 1)
            for c in range(4):
                step.add(V.scalar_tensor_tensor(zn[:, c, :, :], B[0:TS, 5, c * 64:(c + 1) * 64]
                                                .rearrange("p (b h) -> p b h", h=8), 0.125,
                                                view(biasrow[0:TS, :], (0, DEC_B), (1, 8), off=c * 8),
                                                ALU.mult, ALU.add))
            step.wait()
            V.tensor_tensor(zn[:, :, :, :].rearrange("p c b h -> p c (b h)"),
                            zn[:, :, :, :].rearrange("p c b h -> p c (b h)"), view(negn, (0, 4), (1, 64)), ALU.add)\
                .then_inc(zn_ready, 1)
            dve.wait_ge(lnn_ready, 1)
            dve.wait_ge(zn_ready, 1)
            V.scalar_tensor_tensor(spn[0:TS, :, :, :], zn[:, :, :, :], 0.0, lnn[:, :, :, :], ALU.max, ALU.add)\
                .then_inc(spn_ready, 1)
            dve.wait_ge(rn_done, 1)
            V.tensor_tensor(zn[:, :, :, :].rearrange("p a b c -> p (a b c)"),
                            zn[:, :, :, :].rearrange("p a b c -> p (a b c)"), B[0:TS, 6, 0:256], ALU.subtract).then_inc(znr_ready, 1)
            dve.wait_ge(an_ready, 1)
            step.add(V.memset(smask[:, :, :], 1.0))
            step.wait()
            step.add(V.memset(smask[:, :, 0:1], 0.0))

            perm = lambda ap: ap.rearrange("p (s h) -> p h s", h=32)

            def dec_z(group):
                dve.wait_ge(kv_used, group * SLOTS + SLOTS)
                V.scalar_tensor_tensor(zd[:, :, :], perm(B[:, 4, :]), 0.125,
                                       view(biasrow[:, :], (1, 32), (0, 16)), ALU.mult, ALU.add).then_inc(z_ready, 1)

            def dec_sp(b):
                dve.wait_ge(log_ready, b + 1)
                step.add(V.scalar_tensor_tensor(sp17[:, :, 1:17], zd[:, :, :], 0.0, ld[:, :, :], ALU.max, ALU.add))
                step.add(V.tensor_scalar(sp17[:, :, 0:1].rearrange("p (c h) o -> p c (h o)", c=4),
                                         view(spn[:, 0, 0, :], (64, 4), (1, 8), off=b * 8), 1.0, None, ALU.mult))
                step.wait()
                f = "p a b -> p (a b)"
                V.tensor_tensor_scan(inc17[:, :, :].rearrange(f), smask[:, :, :].rearrange(f),
                                     sp17[:, :, :].rearrange(f), 0.0, ALU.mult, ALU.add).then_inc(sp_ready, 1)

            def dec_zr(b):
                dve.wait_ge(r_done, b + 1)
                V.tensor_tensor(ad[:, :, :].rearrange("p a b -> p (a b)"), zd[:, :, :].rearrange("p a b -> p (a b)"),
                                B[:, 5, :], ALU.subtract).then_inc(zr_ready, 1)

            def dec_out(b, group):
                dve.wait_ge(kv_used, group * SLOTS + SLOTS)
                for h2 in range(2):
                    rows = slice(64 * h2, 64 * h2 + 64)
                    V.tensor_scalar(view(bsT[rows, 0, :], (TS, 4), (1, 4), off=b * 4),
                                    view(B[rows, 6, 4 * h2:4 * h2 + 4], (8, 4), (1, 4)), 1.0, None, ALU.mult)\
                        .then_inc(o_taken, 1)

            dec_z(0)
            dec_sp(0)
            with dve.Fori(0, DEC_B - 1) as b, step.loop(b, DEC_B - 1, 2):
                dec_zr(b)
                dve.wait_ge(zr_ready, b + 2)
                dec_z(b * 2 + 1)
                dve.wait_ge(z_ready, b + 2)
                dec_sp(b + 1)
                dec_out(b, b * 2 + 2)
            dec_zr(DEC_B - 1)
            dec_out(DEC_B - 1, 2 * DEC_B - 1)
            dve.wait_ge(bs_hi, 1)
            dve.wait_ge(o_taken, 2 * DEC_B + 2)
            V.tensor_tensor(x_lo[:, 4:8, TP:NT], bsT[:, :, :], x_hi[:, 4:8, TP:NT].bitcast(F32), ALU.subtract)\
                .then_inc(bs_lo, 1)

            PER = 2 * 8
            with dve.Fori(0, 4) as c, step.loop(c, 4, PER):
                dve.wait_ge(pav_done, c * 2 + 1)
                for pair, whole in ((qpair, qT), (kpair, kT)):
                    V.tensor_scalar(pair[:, :], view(whole[:, 0, :], (1, TP), off=c * NT), 1.0, None, ALU.mult)\
                        .then_inc(pk_ready, 1)
                V.tensor_scalar(vpair[:, :, :], view(v_nat[:, 0, :], (512, NB), (1, P), off=c * P), 1.0, None,
                                ALU.mult).then_inc(pk_ready, 1)
                for h2 in range(2):
                    n = c * 2 + h2
                    bias = view(bias8[:, :], (1, 1), off=n)
                    dve.wait_ge(pqk_done, n + 1)
                    dve.wait_ge(pav_done, n + 1)
                    step.add(V.tensor_scalar(zp[:, 0:TP], B[:, 0, :], 0.125, bias, ALU.mult, ALU.add))
                    step.add(V.tensor_scalar(zp[:, TP:ZW].rearrange("p (a n) -> p a n", a=2), B[:, 1:3, 0:384],
                                             0.125, bias, ALU.mult, ALU.add))
                    step.wait()
                    for j in range(NB):
                        last = V.tensor_tensor(zp[:, ZOFF[j]:ZOFF[j] + P], zp[:, ZOFF[j]:ZOFF[j] + P], neg_ge, ALU.add)
                        if j < NB - 1:
                            step.add(last)
                    last.then_inc(pz_ready, 1)
                    dve.wait_ge(pz_ready, n + 2)
                    dve.wait_ge(plog_ready, n + 1)
                    step.add(V.scalar_tensor_tensor(lp[:, :], zp[:, :], 0.0, lp[:, :], ALU.max, ALU.add))
                    step.wait()
                    step.add(V.tensor_tensor(tp1[:, :], lp[:, ZOFF[2] + P:ZOFF[2] + 2 * P],
                                             lp[:, ZOFF[3]:ZOFF[3] + P], ALU.add))
                    step.wait()
                    V.tensor_tensor(tp0[:, 0:P], lp[:, ZOFF[1] + P:ZOFF[1] + 2 * P], lp[:, ZOFF[2]:ZOFF[2] + P],
                                    ALU.add).then_inc(psp_ready, 1)
                    V.tensor_tensor(tp0[:, P:2 * P], lp[:, ZOFF[1] + 2 * P:ZOFF[1] + 3 * P], tp1[:, :],
                                    ALU.add).then_inc(psp_ready, 1)
                    dve.wait_ge(pr_done, n + 1)
                    step.add(V.tensor_tensor(zp[:, 0:TP], zp[:, 0:TP], B[:, 4, :], ALU.subtract))
                    V.tensor_tensor(zp[:, TP:ZW].rearrange("p (a n) -> p a n", a=2),
                                    zp[:, TP:ZW].rearrange("p (a n) -> p a n", a=2), B[:, 5:7, 0:384],
                                    ALU.subtract).then_inc(pzr_ready, 1)
                dve.wait_ge(pav_done, c * 2 + 3)
                hi = view(x_hi[:, 4, 0:TP], (1, TP), off=c * NT)
                lo = view(x_lo[:, 4, 0:TP], (1, TP), off=c * NT)
                V.tensor_scalar(hi, B[:, 3, :], 1.0, None, ALU.mult).then_inc(po_hi, 1)
                dve.wait_ge(po_hi, c + 1)
                V.tensor_tensor(lo, B[:, 3, :], hi.bitcast(F32), ALU.subtract).then_inc(po_lo, 1)

            def add_up(base, n_rows, scaled, k, k_next):
                def body(i, j, kk):
                    if kk:
                        low(i + (base + 2), j, kk)
                    dve.wait_ge(tile_done, i + (base + 1))
                    out = view(y[:, 0, :], (HN, 2), (1, HN), off=i * NT)
                    V.tensor_tensor(out, out, bank_pair(j), ALU.add).then_inc(evicted[j], 1)

                dve.wait_ge(y_scaled, scaled)
                stream(dve, n_rows, k, k_next, body)

            def norm(n):
                half = U_DONE[n] // 2 + 1
                for j in range(2):
                    dve.wait_ge(evicted[j], half)
                step.add(V.tensor_tensor(s1[:, :], y[:, 0, :], y[:, 1, :], ALU.add))
                for m in range(2, KD):
                    step.wait()
                    last = V.tensor_tensor(s1[:, :], s1[:, :], y[:, m, :], ALU.add)
                    if m < KD - 1:
                        step.add(last)
                last.then_inc(s_sum, 1)
                dve.wait_ge(m_done, n + 1)
                for m in range(KD):
                    V.tensor_tensor(halves(y[:, m, :]), halves(y[:, m, :]), B[:, 4:6, 0:HN], ALU.subtract)\
                        .then_inc(c_ready, 1)
                dve.wait_ge(std_ready, n + 1)
                V.reciprocal(std[:, :], std[:, :]).then_inc(rs_ready, 1)
                dve.wait_ge(rs_ready, n * (KD + 1) + 1)
                dve.wait_ge(c_ready, (n + 1) * KD)
                for m in range(KD):
                    V.tensor_tensor(y[:, m, :], y[:, m, :], std[:, :], ALU.mult).then_inc(rs_ready, 1)
                for m in range(KD):
                    dve.wait_ge(lnhi_ready, n * KD + m + 1)
                    V.tensor_tensor(x_lo[:, m, :], y[:, m, :], x_hi[:, m, :].bitcast(F32), ALU.subtract)\
                        .then_inc(ln_done, 1)

            def ffn(l, k_last):
                for half in range(2):
                    base = U_FFN[l] + half * (N_UP + N_OUT)
                    pairs = (2 * l + half) * KF
                    gs = view(gp[:, 0:1], (6, DEC_B), (1, 2), off=TP + 2)

                    def pair(i, k):
                        tile = i + half * KF
                        w = lambda t: view(cw[:, l, 0, :], (1, 1), off=tile * 4 + t)
                        low(i * 2 + (base + 2), 0, k)
                        dve.wait_ge(evicted[0], i + (base // 2 + 2))
                        step.add(V.tensor_scalar(gs, view(cstate[:, l, 0, :], (2, DEC_B), (1, 2), off=tile * 16),
                                                 1.0, None, ALU.mult))
                        step.add(V.tensor_scalar(view(cso[:, l, 0, :], (1, 2), off=tile * 18), gp[:, TP:TP + 2],
                                                 1.0, None, ALU.mult))
                        step.add(V.tensor_scalar(view(cso[:, l, 0, :], (2, DEC_B), (1, 2), off=tile * 18 + 2),
                                                 view(gp[:, 0:1], (6, DEC_B), (1, 2), off=TP + 6), 1.0, None, ALU.mult))
                        step.wait()
                        step.add(V.tensor_scalar(gc[:, :], gp[:, 0:GC], w(0), w(3), ALU.mult, ALU.add))
                        step.wait()
                        step.add(V.scalar_tensor_tensor(gc[:, :], gp[:, 1:GC + 1], w(1), gc[:, :], ALU.mult, ALU.add))
                        step.wait()
                        V.scalar_tensor_tensor(gc[:, :], gp[:, 2:GC + 2], w(2), gc[:, :], ALU.mult, ALU.add)\
                            .then_inc(conv_done, 1)
                        low(i * 2 + (base + 3), 1, k)
                        dve.wait_ge(gelu_ready, i + (pairs + 1))
                        dve.wait_ge(tile_done, i * 2 + (base + 2))
                        step.add(V.tensor_tensor(af[:, 0:HN], ge[:, 0:HN], B[:, 2, 0:HN], ALU.mult))
                        step.add(V.tensor_tensor(af[:, HN:TP], ge[:, HN:TP], B[:, 3, 0:TP - HN], ALU.mult))
                        V.tensor_tensor(af[:, TP:NT].rearrange("p (b t) -> p b t", t=DEC_T),
                                        view(ge[:, 0:1], (6, DEC_B), (1, DEC_T), off=TP + 2),
                                        B[:, 3, TP - HN:HN].rearrange("p (b t) -> p b t", t=DEC_T), ALU.mult)\
                            .then_inc(evicted[1], 1)
                        hi = view(act_hi[:, 0, :], (1, NT), off=i * NT)
                        step.wait()
                        dve.wait_ge(evicted[1], i + (base // 2 + 2))
                        step.add(V.tensor_scalar(hi, af[:, :], 1.0, None, ALU.mult))
                        step.wait()
                        V.tensor_tensor(view(act_lo[:, 0, :], (1, NT), off=i * NT), af[:, :], hi.bitcast(F32),
                                        ALU.subtract).then_inc(act_ready, 1)

                    if half == 0:
                        step.add(V.memset(gp[:, 0:2], 0.0))
                    with dve.Fori(0, KF - 1) as i, step.loop(i, KF - 1, 8):
                        pair(i, KD)
                    pair(KF - 1, KF)
                    add_up(base + N_UP, N_OUT, 1 + KD * (1 + 2 * l), KF, KD if half == 0 else k_last)

            U_DONE = [U_OUT_AB + N_OUT, U_RET, U_FFN[1], U_ALL]
            add_up(U_OUT_AB, N_OUT, 1, KD, KD)
            norm(0)
            dve.wait_ge(stored, 3 * 16)
            ffn(0, KD)
            norm(1)

            dve.wait_ge(y_scaled, 1 + 2 * KD)
            dve.wait_ge(zeroed, 3)
            step.add(V.memset(rmv[:, :, :], 1.0))
            with dve.Fori(0, H_C) as h, step.loop(h, H_C, RET_STEPS):
                base = h * N_RET + U_RET
                for i in range(N_RIN):
                    low(base + (i + 2), i % 2, KD if i < N_RIN - 2 else 4)
                dve.wait_ge(tab_in, h * 16 + 16)
                dve.wait_ge(roped, h * 4 + 4)
                for dt in range(2):
                    V.tensor_tensor(view(qm[:, dt, 0, :], (TS + DEC_T, DEC_B), (1, DEC_T)),
                                    rqk[:, dt, TP:NT].rearrange("p (b t) -> p b t", t=DEC_T),
                                    tab[:, T_QD:T_QD + TS].rearrange("p (b t) -> p b t", t=DEC_T), ALU.mult)\
                        .then_inc(qm_ready, 1)
                for t in range(NB + 1):
                    rows = P if t < NB else TS
                    dve.wait_ge(rt_done, h * (NB + 1) + (t + 1))
                    V.tensor_scalar(rkn[0:rows, t, :], B[0:rows, 4 + t % 2, 0:DK], tab[0:rows, T_KP + t:T_KP + t + 1],
                                    None, ALU.mult).then_inc(rk_ready, 1)
                for j, (bank, c0) in enumerate(((0, 0), (1, 0), (2, 0), (2, 256))):
                    dve.wait_ge(sc_done, h * 3 + min(j + 1, 3))
                    V.tensor_tensor(scT[:, ZOFF[j]:ZOFF[j] + CAUSAL[j]], B[:, bank, c0:c0 + CAUSAL[j]],
                                    tab[:, T_DEC:T_DEC + CAUSAL[j]], ALU.mult).then_inc(sc_ready, 1)
                dve.wait_ge(scs_done, h + 1)
                V.tensor_tensor(scs[:, :], B[0:TS, 3, 0:TS], tab[0:TS, T_SS:T_SS + TS], ALU.mult).then_inc(scs_ready, 1)
                dve.wait_ge(rk_ready, h * (NB + 1) + (NB + 1))
                for n in range(DEC_B + 1):
                    if n < DEC_B:
                        if n >= 2:
                            dve.wait_ge(st_done, h * (DEC_B + 1) + n)
                        V.tensor_scalar(km[:, n % 2, :], rkn[0:TS, NB, :], blockm[:, n:n + 1], None, ALU.mult)\
                            .then_inc(km_ready, 1)
                    dve.wait_ge(st_done, h * (DEC_B + 1) + (n + 1))
                    dve.wait_ge(so_stored[n % SO], h * (16 * (DEC_B + 1) // SO) + 16 * (n // SO + 1))
                    banks = B[:, 4:6, :] if n % 2 == 0 else B[:, 6:8, :]
                    if n == 0:
                        V.tensor_copy(so[:, 0, :, :], banks).then_inc(so_ready, 1)
                    else:
                        V.scalar_tensor_tensor(so[:, n % SO, :, :], s0[:, (n - 1) % S0R, :, :], tab[:, T_CD:T_CD + 1],
                                               banks, ALU.mult, ALU.add).then_inc(so_ready, 1)
                for t in range(NB + 1):
                    rows = P if t else TS
                    s = (t - 1) % (NB + 1)
                    dve.wait_ge(ro_copied, h * (NB + 1) + (t + 1))
                    step.add(V.bn_stats(rst[0:rows, s, :], onat[0:rows, s, :]))
                step.wait()
                apart(dve)
                for t in range(NB + 1):
                    rows = P if t < NB else TS
                    last = V.bn_aggr(rmv[0:rows, t, :], rst[0:rows, t, :])
                    if t < NB:
                        step.add(last)
                last.then_inc(rvar_ready, 1)
                dve.wait_ge(rstd_ready, h + 1)
                step.add(V.reciprocal(rrs[:, :], rrs[:, :]))
                step.wait()
                dve.wait_ge(rvar_ready, h + 1)
                for t in range(NB + 1):
                    s = (t - 1) % (NB + 1)
                    rows = P if s < NB else TS
                    V.tensor_scalar(onat[0:rows, s, :], onat[0:rows, s, :], rmv[0:rows, s, 0:1],
                                    rrs[0:rows, s:s + 1], ALU.subtract, ALU.mult).then_inc(rnorm, 1)
                for et in range(4):
                    gain, shift = (tab[:, T_GN + 4 * g + et:T_GN + 4 * g + et + 1] for g in range(2))
                    dve.wait_ge(rb_done, h * 5 + (et + 2))
                    step.add(V.tensor_scalar(rvT[:, et, TP:NT], B[:, 7, et * TS:(et + 1) * TS], gain, shift,
                                             ALU.mult, ALU.add))
                    V.tensor_scalar(rvT[:, et, 0:TP], B[:, 4 + et % 2, :], gain, shift, ALU.mult, ALU.add)\
                        .then_inc(rg_taken, 1)
                    step.wait()
                    dve.wait_ge(rg_taken, h * 4 + (et + 1))
                    V.tensor_tensor(rvT[:, et, :], rvT[:, et, :], rg[:, et, :], ALU.mult).then_inc(m_ready, 1)
                for et in range(4):
                    dve.wait_ge(mhi_ready, h * 4 + (et + 1))
                    V.tensor_tensor(m_lo[:, et, :], rvT[:, et, :], m_hi[:, et, :].bitcast(F32), ALU.subtract)\
                        .then_inc(mlo_ready, 1)
                for i in range(N_OUT):
                    low(base + (N_RIN + i + 2), i % 2, 4 if i < N_OUT - 2 else KD)
                    dve.wait_ge(tile_done, base + (N_RIN + i + 1))
                    V.tensor_tensor(halves(y[:, i, :]), halves(y[:, i, :]), bank_pair(i % 2), ALU.add)\
                        .then_inc(evicted[i % 2], 1)
            norm(2)
            ffn(1, None)
            norm(3)

        @block.tensor
        def _(pe):
            mm = nc.tensor.matmul

            def product(base, n, k, hi, lo):
                with pe.Fori(0, n // 2) as i:
                    for j in range(2):
                        pe.wait_ge(lo_ready, i * 2 + (base + j + 1))
                        pe.wait_ge(evicted[j], i + (base // 2 + 1))
                        tile_body(j, k, hi, lo)

            def tile_body(j, k, hi, lo):
                for kt in range(k):
                    w = slice(kt * P, (kt + 1) * P)
                    for n, (a, x) in enumerate(((w_hi, hi), (w_hi, lo), (w_lo, hi))):
                        for half in range(2):
                            last = mm(B[:, 2 * j + half, 0:HN], a[:, j, w], x[:, kt, half * HN:(half + 1) * HN],
                                      start=kt == 0 and n == 0, stop=kt == k - 1 and n == 2)
                last.then_inc(tile_done, 1)

            pe.wait_ge(x_ready, 1)
            product(U_IN_AB, N_IN_AB, KD, x_hi, x_lo)

            pe.wait_ge(const_in, 5 * 16)
            for j in range(2):
                pe.wait_ge(evicted[j], N_IN_AB // 2 + 1)
            for t in range(NB + 1):
                rows = P if t < NB else TS
                for first, bank, taken, done in ((0, 4, cop_a, nat_a), (4, 6, cop_b, nat_b)):
                    if t >= 2:
                        pe.wait_ge(taken, t - 1)
                    for f in range(4):
                        last = nc.tensor.transpose(B[0:rows, bank + t % 2, f * P:(f + 1) * P],
                                                   y[:, first + f, t * P:t * P + rows], ident)
                    last.then_inc(done, 1)

            pe.wait_ge(ws_ready, 1)
            pe.wait_ge(va_ready, NB + 1)
            for g in range(8):
                last = mm(B[64 * (g % 2):64 * (g % 2) + 64, 4, (g // 2) * TS:(g // 2 + 1) * TS],
                          va_nat[0:TS, NB, g * 64:(g + 1) * 64], w4[:, g, :], start=True, stop=True)
            last.then_inc(gm_mixed, 1)
            for pr in range(4):
                for g2 in range(2):
                    g = 2 * pr + g2
                    for n in range(NB):
                        last = mm(B[64 * g2:64 * g2 + 64, pr, n * P:(n + 1) * P], va_nat[:, n, g * 64:(g + 1) * 64],
                                  wsT[:, g, :], start=True, stop=True)
                last.then_inc(gm_mixed, 1)

            pe.wait_ge(qbd_ready, 2)
            for c in range(4):
                last = mm(B[0:TS, 5, c * 64:(c + 1) * 64], kT[:, c, TP:NT],
                          qbd[:, c, :, :].rearrange("p b h -> p (b h)"), start=True, stop=True)
            last.then_inc(zn_done, 1)
            pe.wait_ge(spn_ready, 1)
            pe.wait_ge(cop_b, NB + 1)
            mm(B[0:TS, 6, 0:256], tri[0:TS, 0:TS], spn[0:TS, :, :, :].rearrange("p a b c -> p (a b c)"),
               start=True, stop=True).then_inc(rn_done, 1)
            pe.wait_ge(gm_out, 4)
            pe.wait_ge(an_ready, 1)

            def of_b(t, c, b):
                return view(t[:, c, 0, :], (1, 8), off=b * 8)

            def qk(b, group):
                if not isinstance(b, int) or b:
                    pe.wait_ge(z_ready, b)
                for s in range(SLOTS):
                    pe.wait_ge(kv_landed[s], group * 32 + 32)
                    for g in range(PER_SLOT):
                        for c in range(4):
                            col = (PER_SLOT * s + g) * 32 + c * 8
                            last = mm(B[:, 4, col:col + 8], kv[:, s, g, c * P:(c + 1) * P], of_b(qbd, c, b),
                                      start=True, stop=True)
                    last.then_inc(kv_used, 1)

            def suffix(b):
                pe.wait_ge(sp_ready, b + 1)
                pe.wait_ge(zr_ready, b + 1)
                mm(B[:, 5, :], tri, sp17[:, :, 1:17], start=True, stop=False)
                mm(B[:, 5, :], ones, inc17[:, :, 0:16], start=False, stop=True).then_inc(r_done, 1)

            def av(b, group):
                pe.wait_ge(a_ready, b + 1)
                pe.wait_ge(o_taken, b * 2 + 2)
                for c in range(4):
                    mm(B[:, 6, c * 8:(c + 1) * 8], v_nat[0:TS, NB, c * P:(c + 1) * P], of_b(an, c, b),
                       start=c == 0, stop=False, skip_group_check=True)
                for s in range(SLOTS):
                    pe.wait_ge(kv_landed[s], group * 32 + 32)
                    for g in range(PER_SLOT):
                        for c in range(4):
                            last = mm(B[:, 6, c * 8:(c + 1) * 8], kv[:, s, g, c * P:(c + 1) * P],
                                      ad[:, c * 8:(c + 1) * 8, PER_SLOT * s + g], start=False,
                                      stop=s == SLOTS - 1 and g == PER_SLOT - 1, skip_group_check=True)
                    last.then_inc(kv_used, 1)

            qk(0, 0)
            with pe.Fori(0, DEC_B - 1) as b:
                suffix(b)
                qk(b + 1, b * 2 + 1)
                av(b, b * 2 + 2)
            suffix(DEC_B - 1)
            av(DEC_B - 1, 2 * DEC_B - 1)

            zbank = lambda j, c0, w: B[:, min(j, 2), (256 if j == 3 else 0) + c0:(256 if j == 3 else 0) + c0 + w]
            rbank = lambda j, c0, w: B[:, 4 + min(j, 2), (256 if j == 3 else 0) + c0:(256 if j == 3 else 0) + c0 + w]
            pe.wait_ge(bs_lo, 1)
            with pe.Fori(0, 4) as c:
                pe.wait_ge(pk_ready, c * 3 + 3)
                pe.wait_ge(po_lo, c + 1)
                for h2 in range(2):
                    rows = slice(64 * h2, 64 * h2 + 64)
                    n = c * 2 + h2
                    pe.wait_ge(pz_ready, n + 1)
                    for j in range(NB):
                        last = mm(zbank(j, 0, CAUSAL[j]), kpair[rows, j * P:(j + 1) * P],
                                  qpair[rows, j * P:TP], start=True, stop=True)
                    last.then_inc(pqk_done, 1)
                    pe.wait_ge(psp_ready, n * 2 + 2)
                    pe.wait_ge(pzr_ready, n + 1)
                    for j, behind in ((0, ((1, lp[:, ZOFF[1]:ZOFF[1] + P]), (2, tp0[:, :]))),
                                      (1, ((1, lp[:, ZOFF[2]:ZOFF[2] + P]), (2, tp1[:, :]))),
                                      (2, ((1, lp[:, ZOFF[3]:ZOFF[3] + P]),)), (3, ())):
                        last = mm(rbank(j, 0, CAUSAL[j]), tri, lp[:, ZOFF[j]:ZOFF[j] + CAUSAL[j]], start=True,
                                  stop=not behind)
                        for i, (blk, t) in enumerate(behind):
                            last = mm(rbank(j, blk * P, t.shape[1]), ones, t, start=False, stop=i == len(behind) - 1)
                    last.then_inc(pr_done, 1)
                    pe.wait_ge(pa_ready, n + 1)
                    for j in range(NB):
                        last = mm(B[rows, 3, j * P:TP], vpair[:, j, 64 * h2:64 * h2 + 64],
                                  zp[:, ZOFF[j]:ZOFF[j] + CAUSAL[j]], start=j == 0, stop=j == NB - 1)
                    last.then_inc(pav_done, 1)

            def norm(n):
                pe.wait_ge(s_sum, n + 1)
                for half in range(2):
                    last = mm(B[:, 4 + half, 0:HN], mean_mat, s1[:, half * HN:(half + 1) * HN], start=True, stop=True)
                last.then_inc(m_done, 1)
                for m in range(KD):
                    pe.wait_ge(sq_ready, n * KD + m + 1)
                    for half in range(2):
                        last = mm(B[:, 6 + half, 0:HN], mean_mat, sq[:, m % 2, half * HN:(half + 1) * HN],
                                  start=m == 0, stop=m == KD - 1)
                    last.then_inc(sq_used, 1)

            def ffn(l):
                pe.wait_ge(ln_done, (2 * l + 1) * KD)
                for half in range(2):
                    base = U_FFN[l] + half * (N_UP + N_OUT)
                    product(base, N_UP, KD, x_hi, x_lo)
                    pe.wait_ge(act_ready, (2 * l + half + 1) * KF)
                    product(base + N_UP, N_OUT, KF, act_hi, act_lo)

            pe.wait_ge(po_lo, 4 + 1)
            pe.wait_ge(gm_lo, 4)
            product(U_OUT_AB, N_OUT, KD, x_hi, x_lo)
            norm(0)
            ffn(0)
            norm(1)
            pe.wait_ge(ln_done, 2 * KD)
            with pe.Fori(0, H_C) as h:
                with pe.Fori(0, N_RIN // 2) as i:
                    for j in range(2):
                        pe.wait_ge(lo_ready, h * N_RET + (i * 2 + (U_RET + j + 1)))
                        pe.wait_ge(evicted[j], h * (N_RET // 2) + (i + U_RET // 2 + 1))
                        tile_body(j, KD, x_hi, x_lo)
                pe.wait_ge(roped, h * 4 + 4)
                for j in range(2):
                    pe.wait_ge(evicted[j], h * (N_RET // 2) + (U_RET // 2 + N_RIN // 2 + 1))
                for t in range(NB + 1):
                    rows = P if t < NB else TS
                    if t >= 2:
                        pe.wait_ge(rk_ready, h * (NB + 1) + (t - 1))
                    for f in range(2):
                        last = nc.tensor.transpose(B[0:rows, 4 + t % 2, f * P:(f + 1) * P],
                                                   rqk[:, 2 + f, t * P:t * P + rows], ident)
                    last.then_inc(rt_done, 1)
                    if t >= 2:
                        pe.wait_ge(rv_ready, h * (NB + 1) + (t - 1))
                    for f in range(4):
                        last = nc.tensor.transpose(B[0:rows, 6 + t % 2, f * P:(f + 1) * P],
                                                   rvT[:, f, t * P:t * P + rows], ident)
                    last.then_inc(rv_done, 1)
                for j in range(NB):
                    for dt in range(2):
                        last = mm(zbank(j, 0, CAUSAL[j]), rqk[:, 2 + dt, j * P:(j + 1) * P], rqk[:, dt, j * P:TP],
                                  start=dt == 0, stop=dt == 1)
                    if j != 2:
                        last.then_inc(sc_done, 1)
                for dt in range(2):
                    last = mm(B[0:TS, 3, 0:TS], rqk[:, 2 + dt, TP:NT], rqk[:, dt, TP:NT], start=dt == 0, stop=dt == 1)
                last.then_inc(scs_done, 1)
                pe.wait_ge(rk_ready, h * (NB + 1) + (NB + 1))
                pe.wait_ge(rv_ready, h * (NB + 1) + (NB + 1))
                for dt in range(2):
                    for j in range(NB):
                        last = mm(B[:, 4 + dt, :], rkn[:, j, dt * P:(dt + 1) * P], rvn[:, j, :],
                                  start=j == 0, stop=j == NB - 1)
                last.then_inc(st_done, 1)
                pe.wait_ge(scs_ready, h + 1)
                pe.wait_ge(qm_ready, h * 2 + 2)
                apart(pe)
                mm(B[0:TS, 3, :], scs[:, :], rvn[0:TS, NB, :], start=True, stop=False)
                for b in range(DEC_B):
                    pe.wait_ge(s0_landed[b % S0R], h * (16 * DEC_B // S0R) + 16 * (b // S0R + 1))
                    for dt in range(2):
                        last = mm(B[0:TS, 3, :], qm[:, dt, b, :], s0[:, b % S0R, dt, :], start=False,
                                  stop=b == DEC_B - 1 and dt == 1)
                    if b == DEC_B - 1:
                        last.then_inc(ro_done, 1)
                    pe.wait_ge(km_ready, h * DEC_B + (b + 1))
                    if b:
                        pe.wait_ge(so_ready, h * (DEC_B + 1) + b)
                    for dt in range(2):
                        last = mm(B[:, (6 if b % 2 == 0 else 4) + dt, :], km[:, b % 2, dt * P:(dt + 1) * P],
                                  rvn[0:TS, NB, :], start=True, stop=True)
                    last.then_inc(st_done, 1)
                pe.wait_ge(sc_ready, h * 4 + 4)
                for t, bank in enumerate((0, 1, 2, 6)):
                    if t == 3:
                        pe.wait_ge(so_ready, h * (DEC_B + 1) + DEC_B)
                    for j in range(t + 1):
                        c0 = ZOFF[j] + (t - j) * P
                        last = mm(B[:, bank, :], scT[:, c0:c0 + P], rvn[:, j, :], start=j == 0, stop=j == t)
                    last.then_inc(ro_done, 1)
                pe.wait_ge(rnorm, h * 5 + 1)
                pe.wait_ge(so_ready, h * (DEC_B + 1) + (DEC_B + 1))
                apart(pe)
                for et in range(4):
                    last = nc.tensor.transpose(B[:, 7, et * TS:(et + 1) * TS], onat[0:TS, NB, et * P:(et + 1) * P],
                                               ident[0:TS, 0:TS])
                last.then_inc(rb_done, 1)
                for et in range(4):
                    if et >= 2:
                        pe.wait_ge(rg_taken, h * 4 + (et - 1))
                    for t in range(NB):
                        pe.wait_ge(rnorm, h * 5 + (t + 2)) if et == 0 else None
                        last = nc.tensor.transpose(B[:, 4 + et % 2, t * P:(t + 1) * P],
                                                   onat[:, t, et * P:(et + 1) * P], ident)
                    last.then_inc(rb_done, 1)
                pe.wait_ge(mlo_ready, h * 4 + 4)
                apart(pe)
                with pe.Fori(0, N_OUT // 2) as i:
                    for j in range(2):
                        pe.wait_ge(lo_ready, h * N_RET + (i * 2 + (U_RET + N_RIN + j + 1)))
                        pe.wait_ge(evicted[j], h * (N_RET // 2) + (i + (U_RET + N_RIN) // 2 + 1))
                        tile_body(j, 4, m_hi, m_lo)
            norm(2)
            ffn(1)
            norm(3)


RET_STEPS = 14


def decays(h):
    return np.log1p(-(2.0 ** (-5.0 - h)))


def constants():
    i = np.arange(P)
    cst = np.zeros((P, 7, P), np.float32)
    cst[:, 0] = np.eye(P)
    cst[:, 1] = 1.0
    cst[:, 2] = i[:, None] >= i[None, :]
    cst[:, 3] = i[:, None] <= i[None, :]
    cst[:, 4] = np.where(i[:, None] >= i[None, :], MASKED, 0.0)
    cst[:, 5] = 1.0 / D
    r = np.arange(TS)
    col = np.arange(64)
    ok = (r[:, None] // DEC_T == col[None, :] // 8) & (r[:, None] % DEC_T < col[None, :] % DEC_T)
    cst[:TS, 6, 0:64] = np.where(ok, 0.0, MASKED)
    cst[:TS, 6, 64:72] = r[:, None] // DEC_T == np.arange(DEC_B)[None, :]
    cst[:, 6, 72] = EPS
    same = r[:, None] // DEC_T == r[None, :] // DEC_T
    cst[:TS, 6, 80:80 + TS] = same & (r[:, None] <= r[None, :])

    pos = np.concatenate([np.arange(TP), np.tile(PAST + np.arange(DEC_T), DEC_B)]).astype(np.float32)
    inv = np.float32(10000.0) ** (-np.arange(P, dtype=np.float32) / np.float32(P))
    ang = inv[:, None].astype(np.float32) * pos[None, :]
    rope = np.stack([np.cos(ang), np.sin(ang)], 1).astype(np.float32)

    tab = np.zeros((H_C, P, T_W), np.float64)
    for h in range(H_C):
        g = decays(h)
        d = np.arange(TP)[None, :] - i[:, None]
        tab[h, :, T_DEC:T_DEC + TP] = np.where(d >= 0, np.exp(d * g), 0.0) / 16.0
        for j in range(NB):
            tab[h, :, T_KP + j] = np.exp((TP - 1 - (j * P + i)) * g) / 16.0
        tab[h, :TS, T_KS] = np.exp((DEC_T - 1 - r % DEC_T) * g) / 16.0
        tab[h, :, T_QD:T_QD + TS] = np.exp((r % DEC_T + 1) * g)[None, :]
        dd = r[None, :] - r[:, None]
        tab[h, :TS, T_SS:T_SS + TS] = np.where(same & (dd >= 0), np.exp(dd * g), 0.0) / 16.0
        tab[h, :, T_CD] = np.exp(DEC_T * g)
    return cst, rope, tab.astype(np.float32)


def lay_out(x_prompt, x_sample, cache_sb_k, cache_sb_v, state_ret, state_ffn_conv, page_table,
            w_in_ab, vln_g, vln_b, w_s, b_s, sb_bias, w_out_ab, w_in_ret, gn_g, gn_b, w_out_ret,
            ln1_g, ln1_b, ln2_g, ln2_b, w_up, conv_w, conv_b, w_down):
    C = np.ascontiguousarray

    def pack(w, order=None):
        k, m = w.shape
        t = w.reshape(k // P, P, m // P, P).transpose(2, 1, 0, 3).reshape(m // P, P, k)
        return C(t if order is None else t[order])

    cst, rope, tab = constants()
    rows = lambda x: x.reshape(-1, P).T
    gn = np.stack([gn_g[0].reshape(H_C, 4, P), gn_b[0].reshape(H_C, 4, P)], 1)
    tab[:, :, T_GN:T_GN + 8] = gn.transpose(0, 3, 1, 2).reshape(H_C, P, 8)
    xs = np.concatenate([x_prompt[0], x_sample.reshape(TS, D)], 0)
    out = {"xT": C(xs.T.reshape(KD, P, NT).transpose(1, 0, 2)), "cst": cst, "rope": rope, "tab": tab}
    out["w_in_ab"] = pack(w_in_ab[0], [4, 5, 6, 7, 16, 17, 18, 19, 0, 1, 2, 3, 8, 9, 10, 11, 12, 13, 14, 15])
    out["w_out_ab"] = pack(w_out_ab[0])
    gv = [n for t in range(NFF) for n in (t, NFF + t)]
    out["w_up"] = np.concatenate([pack(w_up[l], gv) for l in range(LAYERS)])
    out["w_dn"] = C(w_down.reshape(LAYERS, 2, KF, P, KD, P).transpose(0, 1, 4, 3, 2, 5)
                    .reshape(LAYERS * 2 * KD, P, KF * P))
    out["w_rin"] = pack(w_in_ret[0], [n for h in range(H_C) for n in (
        2 * h, 2 * h + 1, 8 + 2 * h, 9 + 2 * h, *range(16 + 4 * h, 20 + 4 * h), *range(32 + 4 * h, 36 + 4 * h))])
    out["w_rout"] = C(w_out_ret[0].reshape(H_C, 4, P, KD, P).transpose(0, 3, 2, 1, 4).reshape(H_C * KD, P, 4 * P))
    pool = cache_sb_k.shape[1]
    out["kc"] = C(cache_sb_k[0].reshape(pool, P, 4, P).transpose(0, 3, 2, 1).reshape(pool, P, 512))
    out["vc"] = C(cache_sb_v[0].reshape(pool, P, 512))
    out["ptab"] = C(page_table[:, ::-1].reshape(1, DEC_B * N_PAGES))
    out["vlng"] = C(np.broadcast_to(vln_g[0], (P, 512)))
    out["vlnb"] = C(np.broadcast_to(vln_b[0], (P, 512)))
    out["bias8"] = C(np.broadcast_to(sb_bias[0], (P, H_B)))
    out["wsT"] = C(w_s[0].transpose(2, 0, 1))
    out["w4"] = C(np.tile(w_s[0, :, :DEC_T, :DEC_T].transpose(2, 0, 1), (DEC_B, 1, DEC_B)))
    out["brep"] = C(np.repeat(b_s[0].reshape(4, 2, P).transpose(1, 0, 2), 64, 0))
    ln = np.stack([np.stack([ln1_g, ln1_b], 1), np.stack([ln2_g, ln2_b], 1)], 1).reshape(4, 2, KD, P)
    out["lnp"] = C(ln.transpose(3, 0, 1, 2))
    cwb = np.concatenate([conv_w, conv_b[:, None]], 1).reshape(LAYERS, 4, NFF, P)
    out["cw"] = C(cwb.transpose(3, 0, 2, 1))
    out["cstate"] = C(state_ffn_conv.reshape(LAYERS, 2 * DEC_B, NFF, P).transpose(3, 0, 2, 1))
    out["s0"] = C(state_ret[0].reshape(DEC_B, H_C, 2, P, DV).transpose(1, 0, 3, 2, 4)
                  .reshape(H_C * DEC_B, P, 2 * DV))
    return out


OUTS = {"yT": (P, KD, NT), "kT": (P, 4, NT), "vT": (P, 4, NT), "chunk_v": (TS, 512),
        "ret_p": (H_C, P, 2 * DV), "ret_s": (H_C * DEC_B, P, 2 * DV), "conv_out": (LAYERS, P, NFF * 18)}


def give_back(o):
    C = np.ascontiguousarray
    yt = o["yT"].transpose(2, 1, 0).reshape(NT, D)
    kt = o["kT"].transpose(2, 1, 0).reshape(NT, 512)
    vt = o["vT"].transpose(2, 1, 0).reshape(NT, 512)
    cv = o["conv_out"].reshape(LAYERS, P, NFF, 18)
    conv_p = cv[..., 0:2].transpose(0, 3, 2, 1).reshape(LAYERS, 1, 2, DFF)
    conv_s = cv[..., 2:].reshape(LAYERS, P, NFF, DEC_B, 2).transpose(0, 3, 4, 2, 1).reshape(LAYERS, DEC_B, 2, DFF)
    rp = o["ret_p"].reshape(1, 1, H_C, P, 2, DV).transpose(0, 1, 2, 4, 3, 5).reshape(1, 1, H_C, DK, DV)
    rs = o["ret_s"].reshape(H_C, DEC_B, P, 2, DV).transpose(1, 0, 3, 2, 4).reshape(1, DEC_B, H_C, DK, DV)
    return tuple(C(a) for a in (
        yt[:TP].reshape(1, TP, D), yt[TP:].reshape(DEC_B, DEC_T, D),
        kt[:TP].reshape(1, 1, NB, P, H_B, DH_B), vt[:TP].reshape(1, 1, NB, P, H_B, DH_B),
        kt[TP:].reshape(1, DEC_B, DEC_T, H_B, DH_B), vt[TP:].reshape(1, DEC_B, DEC_T, H_B, DH_B),
        o["chunk_v"].reshape(1, DEC_B, DEC_T, 8, 64), rp, rs, conv_p, conv_s))


def kernel(**inputs):
    import concourse.bacc as bacc
    from concourse.bass_utils import run_bass_kernel_spmd

    arrays = lay_out(**{k: np.asarray(v) for k, v in inputs.items()})
    nc = bacc.Bacc("TRN2", target_bir_lowering=False, num_devices=1)
    A = {n: nc.dram_tensor("in_" + n, a.shape, mybir.dt.from_np(a.dtype), kind="ExternalInput").ap()
         for n, a in arrays.items()}
    for n, shape in OUTS.items():
        A[n] = nc.dram_tensor("out_" + n, shape, F32, kind="ExternalOutput").ap()
    build_program(nc, A)
    r = run_bass_kernel_spmd(nc, [{"in_" + n: a for n, a in arrays.items()}], core_ids=[0])
    return give_back({n: r.results[0]["out_" + n] for n in OUTS})
```

```python
from contextlib import ExitStack, contextmanager

import numpy as np

import concourse.bass as bass
from concourse import mybir

F32 = mybir.dt.float32
F32R = mybir.dt.float32r
I32 = mybir.dt.int32
ALU = mybir.AluOpType
ACT = mybir.ActivationFunctionType

P = 128
D = 1024
KD = D // P
TP, DEC_B, DEC_T = 512, 8, 4
TS = DEC_B * DEC_T
NT = TP + TS
HN = NT // 2
NB = TP // P
PAST = 2048
N_PAGES = PAST // P
LAYERS = 2
DFF = 2816
NFF = DFF // P
KF = NFF // 2
H_B, DH_B = 8, 64
H_C, DK, DV = 4, 256, 512
ALPHA = float((2 * LAYERS) ** 0.25)
EPS = 1e-5
MASKED = -1.0e30
GP = TP + 2 + DEC_B * (DEC_T + 2)
GC = GP - 2
CAUSAL = [TP - P * j for j in range(NB)]
ZOFF = [sum(CAUSAL[:j]) for j in range(NB)]
ZW = sum(CAUSAL)
SLOTS = 8
PER_SLOT = N_PAGES // SLOTS

N_IN_AB, N_OUT, N_UP, N_RIN = 20, KD, 2 * KF, 12
U_IN_AB = 0
U_OUT_AB = U_IN_AB + N_IN_AB
N_FFN = 2 * (N_UP + N_OUT)
N_RET = N_RIN + N_OUT
U_RET = U_OUT_AB + N_OUT + N_FFN
U_FFN = [U_OUT_AB + N_OUT, U_RET + H_C * N_RET]
U_ALL = U_FFN[1] + N_FFN

T_DEC = 0
T_KP = T_DEC + TP
T_KS = T_KP + NB
T_QD = T_KS + 1
T_SS = T_QD + TS
T_CD = T_SS + TS
T_GN = T_CD + 1
T_W = T_GN + 8
RING = 7


class Count:

    def __init__(self, engine, sem):
        self.engine, self.sem, self.n, self.loops = engine, sem, 0, []

    def add(self, instruction):
        instruction.then_inc(self.sem, 1)
        self.n += 1

    def wait(self):
        value = self.n
        for reg, per in self.loops:
            value = reg * per + value
        self.engine.wait_ge(self.sem, value)

    @contextmanager
    def loop(self, reg, times, per):
        first = self.n
        self.loops.append((reg, per))
        yield
        self.loops.pop()
        assert self.n - first == per, f"{self.n - first} steps a turn, not {per}"
        self.n = first + per * times


def uses(slot):
    return sum(b % RING == slot for b in range(DEC_B)) or 1


def view(ap, *dims, off=0):
    return bass.AP(ap.tensor, ap.offset + off, [list(ap.ap[0])] + [list(d) for d in dims])


def halves(ap):
    return ap.rearrange("p (a n) -> p a n", a=2)


def build_program(nc, A):
    with ExitStack() as ctx:
        def sb(name, shape, dt=F32):
            return ctx.enter_context(nc.sbuf_tensor(name, shape, dt))

        def sem(name):
            return ctx.enter_context(nc.semaphore(name))

        def overlay(*tensors):
            with ExitStack() as s:
                return [s.enter_context(nc.sbuf_tensor(n, shape, *(dt or [F32]))) for n, shape, *dt in tensors]

        x_hi = sb("x_hi", [P, KD, NT], F32R)
        x_lo = sb("x_lo", [P, KD, NT], F32R)
        y = sb("y", [P, KD, NT])
        w_raw = sb("w_raw", [P, 2, KF * P])
        w_hi = sb("w_hi", [P, 2, KF * P], F32R)
        w_lo = sb("w_lo", [P, 2, KF * P], F32R)
        cst = sb("cst", [P, 7, P])
        ident, ones, tri, mask_le, neg_ge, mean_mat = (cst[:, i, :] for i in range(6))
        negn = cst[0:TS, 6, 0:64]
        blockm = cst[0:3 * TS, 6, 64:72]
        eps = cst[:, 6, 72:73]
        lnp = sb("lnp", [P, 4, 2, KD])
        cw = sb("cw", [P, LAYERS, NFF, 4])
        cstate = sb("cstate", [P, LAYERS, NFF, 2 * DEC_B])
        cso = sb("cso", [P, LAYERS, NFF, 2 + 2 * DEC_B])
        s1 = sb("s1", [P, NT])
        vp, km, qm = overlay(("vp", [3 * TS, DV], F32R), ("km", [3 * TS, 2, DK], F32R), ("qm", [P, 2, DEC_B, TS]))
        std = sb("std", [P, NT])
        sq = sb("sq", [P, 2, NT])
        ptab = sb("ptab", [1, DEC_B * N_PAGES], I32)
        B = ctx.enter_context(nc.psum_tensor("banks", [P, 8, 512], F32))

        with ExitStack() as mixer0:
            qT, kT, v_nat, qbd, bias8, biasrow, spn, an, bsT, qz, z4, zd, ld, kv = [
                mixer0.enter_context(nc.sbuf_tensor(n, s, F32)) for n, s in (
                    ("qT", [P, 4, NT]), ("kT", [P, 4, NT]), ("v_nat", [P, NB + 1, 512]),
                    ("qbd", [P, 4, DEC_B, 8]), ("bias8", [P, H_B]), ("biasrow", [P, 32]),
                    ("spn", [P, 4, DEC_B, 8]), ("an", [TS, 4, DEC_B, 8]), ("bsT", [P, 4, TS]),
                    ("qz", [P, 4, 32]), ("z4", [P, 4, P]), ("zd", [P, 32, 16]), ("ld", [P, 32, 16]),
                    ("kv", [P, SLOTS, PER_SLOT, 512]))]
            uT, va_nat, wsT, w4, brep, vlng, vlnb, vst, vmv, vrs, gmix, zn, lnn = overlay(
                ("uT", [P, 4, NT]), ("va_nat", [P, NB + 1, 512]),
                ("wsT", [P, 8, P]), ("w4", [TS, 8, TS]), ("brep", [P, 4, P]), ("vlng", [P, 512]),
                ("vlnb", [P, 512]), ("vst", [P, NB + 1, 6]), ("vmv", [P, NB + 1, 2]), ("vrs", [P, NB + 1]),
                ("gmix", [P, NT]), ("zn", [TS, 4, DEC_B, 8]), ("lnn", [TS, 4, DEC_B, 8]))
            sp17, inc17, smask, ad, o32, zp, lp, tp1, tp0, qpair, kpair, vpair = overlay(
                ("sp17", [P, 32, 17]), ("inc17", [P, 32, 17]),
                ("smask", [P, 32, 17]), ("ad", [P, 32, 16]),
                ("o32", [32, 512]),
                ("zp", [P, ZW]), ("lp", [P, ZW]), ("tp1", [P, P]), ("tp0", [P, 2 * P]),
                ("qpair", [P, TP]), ("kpair", [P, TP]), ("vpair", [P, NB, P]))
        act_hi, act_lo, gp, gc, ge, af = overlay(
            ("act_hi", [P, KF, NT], F32R), ("act_lo", [P, KF, NT], F32R), ("gp", [P, GP]), ("gc", [P, GC]),
            ("ge", [P, GC]), ("af", [P, NT]))
        rqk, rvT, rg, rkn, rvn, scT, scs, tab, rope, onat, m_lo, s0, kp, rst, rmv, rrs = overlay(
            ("rqk", [P, 4, NT]), ("rvT", [P, 4, NT]), ("rg", [P, 4, NT]), ("rkn", [P, NB + 1, DK]),
            ("rvn", [P, NB + 1, DV]), ("scT", [P, ZW]), ("scs", [TS, TS]), ("tab", [P, T_W]),
            ("rope", [P, 2, NT]), ("onat", [P, NB + 1, DV]), ("m_lo", [P, 4, NT], F32R),
            ("s0", [P, RING + 1, 2, DV]), ("kp", [3 * TS, DK], F32R),
            ("rst", [P, NB + 1, 6]), ("rmv", [P, NB + 1, 2]), ("rrs", [P, NB + 1]))
        m_hi, = overlay(("m_hi", [P, 4, NT], F32R))
        ropet = onat[:, :, :].rearrange("p a n -> p (a n)")

        w_landed = [sem("w_landed_0"), sem("w_landed_1")]
        hi_ready, lo_ready, tile_done = sem("w_hi_ready"), sem("w_lo_ready"), sem("tile_done")
        evicted = [sem("tile_evicted_0"), sem("tile_evicted_1")]
        const_in, mix_in = sem("const_in"), sem("mixer_const_in")
        x_in = [sem(f"x_in_{n}") for n in range(KD // 2)]
        x_hi_ready, x_lo_ready = sem("x_hi_ready"), sem("x_lo_ready")
        d_step, a_step, g_step = sem("vector_step"), sem("scalar_step"), sem("pool_step")
        nat_a, nat_b, cop_a, cop_b = (sem(n) for n in ("va_transposed", "v_transposed", "va_copied", "v_copied"))
        va_var, va_std, va_ready, ws_ready = (sem(n) for n in ("va_var", "va_std", "va_normed", "ws_masked"))
        gm_mixed, gm_out, gm_hi, gm_lo = (sem(n) for n in ("gmlp_mixed", "gmlp_gated", "gmlp_hi", "gmlp_lo"))
        zeroed, qbd_ready = sem("zeroed"), sem("qbd_ready")
        zn_done, zn_ready, lnn_ready, spn_ready, rn_done, znr_ready, an_ready = (
            sem("new_" + n) for n in ("z_done", "z_ready", "log_ready", "sp_ready", "r_done", "zr_ready", "a_ready"))
        kv_landed = [sem(f"kv_landed_{s}") for s in range(SLOTS)]
        kv_used = sem("kv_slot_used")
        z_ready, log_ready, sp_ready, r_done, zr_ready, a_ready, o_taken = (
            sem("dec_" + n) for n in ("z_ready", "log_ready", "sp_ready", "r_done", "zr_ready", "a_ready", "o_taken"))
        qz_ready, z4_ready, zt_done, o32_ready, o_done = (
            sem("dec_" + n) for n in ("q_ready", "z_rows_ready", "z_transposed", "o_rows_ready", "o_done"))
        bs_hi, bs_lo = sem("dec_out_hi"), sem("dec_out_lo")
        pk_ready, pqk_done, pz_ready, plog_ready, psp_ready, pr_done, pzr_ready, pa_ready, pav_done, po_hi, po_lo = (
            sem("pr_" + n) for n in ("kv_ready", "qk_done", "z_ready", "log_ready", "sp_ready", "r_done",
                                     "zr_ready", "a_ready", "av_done", "o_hi", "o_lo"))
        y_loaded, y_scaled = sem("residual_loaded"), sem("residual_scaled")
        s_sum, m_done, c_ready, sq_ready, sq_used, std_ready, scaled, lnhi_ready, ln_done, y_final = (
            sem("ln_" + n) for n in ("sum_ready", "mean_done", "centred", "square_ready", "square_used",
                                     "first_inv_std_ready", "scaled", "hi_ready", "lo_ready", "shifted"))
        conv_done, gelu_ready, act_ready = sem("conv_done"), sem("gelu_ready"), sem("act_ready")
        roped, rt_done, rk_ready, rv_ready = sem("roped"), sem("ret_transposed"), sem("ret_k_ready"), sem("ret_v_ready")
        rv_done = sem("ret_v_transposed")
        qm_ready = sem("ret_q_decayed")
        sc_done, sc_ready, scs_done, scs_ready = (sem("ret_" + n) for n in (
            "scores_done", "scores_ready", "sample_scores_done", "sample_scores_ready"))
        st_done, so_ready = sem("state_done"), sem("state_out_ready")
        s0_landed = [sem(f"state_landed_{s}") for s in range(RING)]
        so_stored = [sem(f"state_stored_{s}") for s in range(RING + 1)]
        km_ready, kp_hi, kp_ready, vp_hi, vp_ready = (sem("ret_" + n) for n in (
            "k_masked", "k_parts_hi", "k_parts_ready", "v_parts_hi", "v_parts_ready"))
        ro_done, ro_copied, rvar_ready, rstd_ready, rnorm = (sem("ret_" + n) for n in (
            "o_done", "o_copied", "var_ready", "std_ready", "o_normed"))
        rb_done, rg_taken, m_ready, mhi_ready, mlo_ready = (sem("ret_" + n) for n in (
            "o_back", "o_back_taken", "gated", "gated_hi", "gated_lo"))
        tab_in, rope_in = sem("ret_table_in"), sem("rope_in")
        stored, chunk_stored, y_stored = sem("stored"), sem("chunk_v_stored"), sem("y_stored")
        turns = sem("turns")

        block = ctx.enter_context(nc.Block())

        def bank_pair(j):
            return B[:, 2 * j:2 * j + 2, 0:HN]

        def apart(e):
            e.sem_inc(turns, 1)

        def stream(e, n, k, k_next, body):
            with e.Fori(0, n // 2 - 1) as i:
                for j in range(2):
                    body(i * 2 + j, j, k)
            for j in range(2):
                body(n - 2 + j, j, k_next)

        @block.sync
        def _(sp):
            def load(dram, local, u, j, k):
                sp.wait_ge(lo_ready, u - 1)
                sp.dma_start(w_raw[:, j, 0:k * P], dram[bass.ds(local, 1)].rearrange("o p k -> (o p) k"))\
                    .then_inc(w_landed[j], 16)

            def load_all(dram, first, base, n, k, skip=0):
                with sp.Fori(skip // 2, n // 2) as i:
                    for j in range(2):
                        load(dram, i * 2 + (first + j), i * 2 + (base + j), j, k)

            sp.dma_start(w_raw[:, 0, 0:KD * P], A["w_in_ab"][0]).then_inc(w_landed[0], 16)
            for n in range(KD // 2):
                sp.dma_start(y[:, 2 * n:2 * n + 2, :], A["xT"][:, 2 * n:2 * n + 2, :]).then_inc(x_in[n], 16)
            sp.dma_start(w_raw[:, 1, 0:KD * P], A["w_in_ab"][1]).then_inc(w_landed[1], 16)
            load(A["w_in_ab"], 2, U_IN_AB + 2, 0, KD)
            sp.dma_start(cst[:, :, :], A["cst"]).then_inc(const_in, 16)
            sp.dma_start(ptab[:, :], A["ptab"]).then_inc(const_in, 16)
            for dst, name in ((lnp[:, :, :, :], "lnp"), (cw[:, :, :, :], "cw"), (cstate[:, :, :, :], "cstate")):
                sp.dma_start(dst, A[name]).then_inc(const_in, 16)
            load(A["w_in_ab"], 3, U_IN_AB + 3, 1, KD)
            for dst, name in ((wsT[:, :, :], "wsT"), (w4[:, :, :], "w4"), (brep[:, :, :], "brep"),
                              (vlng[:, :], "vlng"), (vlnb[:, :], "vlnb"), (bias8[:, :], "bias8")):
                sp.dma_start(dst, A[name]).then_inc(mix_in, 16)

            def page_ids(b, first):
                _, pages = nc.values_load_multi_w_load_instructions(
                    ptab[0:1, bass.ds(b * N_PAGES + first * PER_SLOT, N_PAGES // 2)],
                    engines=[mybir.EngineType.SP], min_val=0, max_val=A["kc"].shape[0] - 1)
                return pages

            def load_slot(cache, s, pages):
                for g in range(PER_SLOT):
                    sp.dma_start(kv[:, s, g, :], cache[bass.ds(pages[g], 1)].rearrange("o p k -> (o p) k"))\
                        .then_inc(kv_landed[s], 16)

            def load_kv(cache, b, group):
                for first in range(0, SLOTS, SLOTS // 2):
                    pages = page_ids(b, first)
                    for s in range(first, first + SLOTS // 2):
                        sp.wait_ge(kv_used, group * SLOTS + (s + 1 - SLOTS))
                        load_slot(cache, s, pages[(s - first) * PER_SLOT:])

            load_all(A["w_in_ab"], 0, U_IN_AB, N_IN_AB - SLOTS, KD, skip=4)
            sp.wait_ge(const_in, 5 * 16)
            for first in range(0, SLOTS, SLOTS // 2):
                pages = page_ids(0, first)
                for s in range(first, first + SLOTS // 2):
                    u = N_IN_AB - SLOTS + s
                    load(A["w_in_ab"], u, U_IN_AB + u, u % 2, KD)
                    load_slot(A["kc"], s, pages[(s - first) * PER_SLOT:])
            load_all(A["w_out_ab"], 0, U_OUT_AB, 2, KD)
            with sp.Fori(0, DEC_B - 1) as b:
                load_kv(A["kc"], b + 1, b * 2 + 1)
                load_kv(A["vc"], b, b * 2 + 2)
            load_kv(A["vc"], DEC_B - 1, 2 * DEC_B - 1)
            load_all(A["w_out_ab"], 0, U_OUT_AB, N_OUT, KD, skip=2)

            def load_ffn(l):
                for half in range(2):
                    base = U_FFN[l] + half * (N_UP + N_OUT)
                    load_all(A["w_up"], (2 * l + half) * N_UP, base, N_UP, KD)
                    load_all(A["w_dn"], (2 * l + half) * N_OUT, base + N_UP, N_OUT, KF)

            load_ffn(0)
            with sp.Fori(0, H_C) as h:
                base = h * N_RET + U_RET
                for i in range(N_RIN):
                    load(A["w_rin"], h * N_RIN + i, base + i, i % 2, KD)
                for i in range(2):
                    load(A["w_rout"], h * N_OUT + i, base + (N_RIN + i), i % 2, 4)
                sp.dma_start(tab[:, :], A["tab"][bass.ds(h, 1)].rearrange("o p k -> (o p) k")).then_inc(tab_in, 16)

                def load_state(b):
                    slot, before = b % RING, b // RING
                    sp.wait_ge(so_stored[slot], h * (16 * uses(slot)) + 16 * (before + 1))
                    sp.dma_start(s0[:, slot, :, :].rearrange("p a n -> p (a n)"),
                                 A["s0"][bass.ds(h * DEC_B + b, 1)].rearrange("o p k -> (o p) k"))\
                        .then_inc(s0_landed[slot], 16)

                def store_state(n):
                    slot = (n - 1) % RING if n else RING
                    sp.wait_ge(so_ready, h * (DEC_B + 1) + (n + 1))
                    dst = A["ret_p"][bass.ds(h, 1)] if n == 0 else A["ret_s"][bass.ds(h * DEC_B + (n - 1), 1)]
                    sp.dma_start(dst.rearrange("o p k -> (o p) k"),
                                 s0[:, slot, :, :].rearrange("p a n -> p (a n)")).then_inc(so_stored[slot], 16)

                for b in range(RING):
                    load_state(b)
                for n in range(DEC_B + 1):
                    store_state(n)
                    if n >= 2 and n - 2 + RING < DEC_B:
                        load_state(n - 2 + RING)
                for i in range(2, N_OUT):
                    load(A["w_rout"], h * N_OUT + i, base + (N_RIN + i), i % 2, 4)
            load_ffn(1)
            for m in range(KD):
                sp.wait_ge(y_final, m + 1)
                sp.dma_start(A["yT"][:, m, :], y[:, m, :]).then_inc(y_stored, 16)
            sp.wait_ge(y_stored, KD * 16)
            sp.wait_ge(chunk_stored, 16)
            sp.wait_ge(stored, 4 * 16)
            for n in range(RING + 1):
                sp.wait_ge(so_stored[n], 16 * H_C * uses(n) + 16)

        @block.gpsimd
        def _(pool):
            step = Count(pool, g_step)
            nc.gpsimd.memset(qbd[:, :, :, :], 0.0).then_inc(zeroed, 1)
            nc.gpsimd.memset(spn[:, :, :, :], 0.0).then_inc(zeroed, 1)
            for j in range(2):
                pool.wait_ge(evicted[j], (U_IN_AB + 8) // 2 + 1)
            pool.dma_start(A["vT"], y[:, 4:8, :]).then_inc(stored, 16)
            pool.wait_ge(nat_a, NB + 1)
            pool.wait_ge(nat_b, NB + 1)
            pool.wait_ge(stored, 16)
            pool.dma_start(y[:, :, :], A["xT"]).then_inc(y_loaded, 16)
            pool.wait_ge(va_ready, NB + 1)
            pool.dma_start(A["chunk_v"], va_nat[0:TS, NB, :]).then_inc(chunk_stored, 16)
            pool.wait_ge(y_loaded, 16)
            nc.gpsimd.tensor_scalar(y[:, :, :], y[:, :, :], ALPHA, None, ALU.mult).then_inc(y_scaled, 1)
            for j in range(2):
                pool.wait_ge(evicted[j], N_IN_AB // 2 + 1)
            pool.dma_start(A["kT"], kT[:, :, :]).then_inc(stored, 16)

            def scale_residual(n):
                for m in range(KD):
                    pool.wait_ge(ln_done, n * KD + m + 1)
                    nc.gpsimd.tensor_scalar(y[:, m, :], y[:, m, :], lnp[:, n, 1, m:m + 1], ALPHA, ALU.add, ALU.mult)\
                        .then_inc(y_scaled, 1)

            scale_residual(0)
            pool.wait_ge(y_scaled, 1 + KD)
            scale_residual(1)
            pool.wait_ge(y_scaled, 1 + 2 * KD)
            pool.dma_start(rope[:, :, :], A["rope"]).then_inc(rope_in, 16)
            nc.gpsimd.memset(qm[:, :, :, :], 0.0).then_inc(zeroed, 1)
            pool.wait_ge(rope_in, 16)
            with pool.Fori(0, H_C) as h, step.loop(h, H_C, 8):
                for qk in range(2):
                    for j in range(2):
                        pool.wait_ge(evicted[j], h * (N_RET // 2) + (U_RET // 2 + qk + 2))
                    x1, x2 = rqk[:, 2 * qk, :], rqk[:, 2 * qk + 1, :]
                    t = [ropet[:, n * NT:(n + 1) * NT] for n in range(4)]
                    for n, (a, c) in enumerate(((x1, 0), (x2, 1), (x2, 0), (x1, 1))):
                        step.add(nc.gpsimd.tensor_tensor(t[n], a, rope[:, c, :], ALU.mult))
                    step.wait()
                    nc.gpsimd.tensor_tensor(x1, t[0], t[1], ALU.subtract).then_inc(roped, 1)
                    nc.gpsimd.tensor_tensor(x2, t[2], t[3], ALU.add).then_inc(roped, 1)
                    pool.wait_ge(roped, h * 4 + (2 * qk + 2))
                pool.wait_ge(kp_ready, h + 1)
                apart(pool)
                for b in range(DEC_B):
                    if b >= 2:
                        pool.wait_ge(st_done, h * (DEC_B + 1) + b)
                        apart(pool)
                    nc.gpsimd.tensor_scalar(km[:, b % 2, :], kp[:, :].bitcast(F32), blockm[:, b:b + 1], None,
                                            ALU.mult).then_inc(km_ready, 1)
            scale_residual(2)
            for l in range(LAYERS):
                pool.wait_ge(conv_done, 2 * KF * (l + 1) + 1)
                pool.dma_start(A["conv_out"][l], cso[:, l, :, :].rearrange("p a n -> p (a n)")).then_inc(stored, 16)

        @block.scalar
        def _(act):
            step = Count(act, a_step)

            def copy(out, in_):
                return nc.scalar.activation(out, in_, ACT.Copy)

            def split(u, j, k):
                act.wait_ge(w_landed[j], (u - j) * 8 + 16)
                act.wait_ge(tile_done, u - 1)
                copy(w_hi[:, j, 0:k * P], w_raw[:, j, 0:k * P]).then_inc(hi_ready, 1)

            def first_split(j):
                act.wait_ge(w_landed[j], 16)
                copy(w_hi[:, j, 0:KD * P], w_raw[:, j, 0:KD * P]).then_inc(hi_ready, 1)

            nc.scalar.preload_act_table_set("gelu_apprx_tanh_and_others")
            first_split(0)
            for m in range(KD):
                act.wait_ge(x_in[m // 2], 16)
                copy(x_hi[:, m, :], y[:, m, :]).then_inc(x_hi_ready, 1)
            first_split(1)
            act.wait_ge(x_lo_ready, KD)
            act.wait_ge(x_hi_ready, KD)

            def evict_ab(base, dst, d0, func):
                with act.Fori(0, 2) as i:
                    for j in range(2):
                        split(i * 2 + (base + j + 2), j, KD)
                        nc.scalar.activation(halves(view(dst[:, 0, :], (1, NT), off=(i * 2 + (d0 + j)) * NT)),
                                             bank_pair(j), func).then_inc(evicted[j], 1)

            evict_ab(0, y, 0, ACT.Gelu_apprx_tanh)
            evict_ab(4, y, 4, ACT.Copy)
            for t in range(NB + 1):
                rows = P if t < NB else TS
                act.wait_ge(nat_a, t + 1)
                copy(va_nat[0:rows, t, :], B[0:rows, 4 + t % 2, :]).then_inc(cop_a, 1)
            act.wait_ge(const_in, 5 * 16)
            act.wait_ge(va_var, 1)
            nc.scalar.activation(vrs[:, :], vmv[:, :, 1], ACT.Sqrt, bias=eps).then_inc(va_std, 1)
            nc.scalar.preload_act_table_set("gelu_apprx_tanh_and_others")
            evict_ab(8, uT, 0, ACT.Gelu_apprx_tanh)
            evict_ab(12, qT, 0, ACT.Copy)
            evict_ab(16, kT, 0, ACT.Copy)

            def log_part(z, l, ready, n, done):
                act.wait_ge(ready, n)
                step.add(nc.scalar.activation(l, z, ACT.Abs))
                step.wait()
                step.add(nc.scalar.activation(l, l, ACT.Exp, scale=-1.0))
                step.wait()
                nc.scalar.activation(l, l, ACT.Ln, bias=1.0).then_inc(done, 1)

            nc.scalar.preload_act_table_set("natural_log_exp_and_others")
            flat = "p a b c -> p (a b c)"
            log_part(zn[:, :, :, :].rearrange(flat), lnn[:, :, :, :].rearrange(flat), zn_ready, 1, lnn_ready)
            zf, lf, af_ = (t[:, :, :].rearrange("p a b -> p (a b)") for t in (zd, ld, ad))
            for pr in range(4):
                act.wait_ge(gm_out, pr + 1)
                copy(x_hi[:, pr, :], uT[:, pr, :]).then_inc(gm_hi, 1)
                if pr == 2:
                    log_part(zf, lf, z_ready, 1, log_ready)
            act.wait_ge(znr_ready, 1)
            nc.scalar.activation(an[:, :, :, :], zn[:, :, :, :], ACT.Exp).then_inc(an_ready, 1)

            def attend(b, last):
                act.wait_ge(zr_ready, b + 2)
                nc.scalar.activation(af_, af_, ACT.Exp).then_inc(a_ready, 1)
                log_part(zp[:, :], lp[:, :], pz_ready, b + 1, plog_ready)
                act.wait_ge(pzr_ready, b + 2)
                nc.scalar.activation(zp[:, :], zp[:, :], ACT.Exp).then_inc(pa_ready, 1)
                if not last:
                    log_part(zf, lf, z_ready, b + 2, log_ready)

            with act.Fori(0, DEC_B - 1) as b, step.loop(b, DEC_B - 1, 4):
                attend(b, False)
            attend(DEC_B - 1, True)
            act.wait_ge(o_taken, 2 * DEC_B + 2)
            copy(x_hi[:, 4:8, TP:NT], bsT[:, :, :]).then_inc(bs_hi, 1)

            def splits(base, n, k, k_next):
                stream(act, n, k, k_next, lambda i, j, kk: split(i + (base + 2), j, kk))

            def norm(n):
                nc.scalar.preload_act_table_set("natural_log_exp_and_others")
                for m in range(KD):
                    act.wait_ge(c_ready, n * KD + m + 1)
                    if m >= 2:
                        act.wait_ge(sq_used, n * KD + m - 1)
                    nc.scalar.activation(sq[:, m % 2, :], y[:, m, :], ACT.Square).then_inc(sq_ready, 1)
                act.wait_ge(sq_used, n * KD + KD)
                step.add(nc.scalar.activation(halves(std[:, :]), B[:, 6:8, 0:HN], ACT.Ln, bias=eps))
                step.wait()
                nc.scalar.activation(std[:, :], std[:, :], ACT.Exp, scale=-0.5).then_inc(std_ready, 1)
                for m in range(KD):
                    act.wait_ge(scaled, n * KD + m + 1)
                    shift = lnp[:, n, 1, m:m + 1]
                    if n < 3:
                        nc.scalar.activation(x_hi[:, m, :], y[:, m, :], ACT.Identity, bias=shift)\
                            .then_inc(lnhi_ready, 1)
                    else:
                        nc.scalar.activation(y[:, m, :], y[:, m, :], ACT.Identity, bias=shift).then_inc(y_final, 1)

            def ffn(l, k_last):
                nc.scalar.preload_act_table_set("gelu_apprx_tanh_and_others")
                for half in range(2):
                    base = U_FFN[l] + half * (N_UP + N_OUT)
                    pairs = (2 * l + half) * KF

                    def pair(i, k):
                        split(i * 2 + (base + 2), 0, k)
                        act.wait_ge(conv_done, i + (pairs + 1))
                        step.add(copy(gp[:, 2:2 + HN], B[:, 0, 0:HN]))
                        step.add(copy(gp[:, 2 + HN:2 + TP], B[:, 1, 0:TP - HN]))
                        copy(view(gp[:, 0:1], (6, DEC_B), (1, DEC_T), off=TP + 4),
                             B[:, 1, TP - HN:HN].rearrange("p (b t) -> p b t", t=DEC_T)).then_inc(evicted[0], 1)
                        split(i * 2 + (base + 3), 1, k)
                        act.wait_ge(conv_done, i + (pairs + 2))
                        nc.scalar.activation(ge[:, :], gc[:, :], ACT.Gelu_apprx_tanh).then_inc(gelu_ready, 1)

                    with act.Fori(0, KF - 1) as i, step.loop(i, KF - 1, 2):
                        pair(i, KD)
                    pair(KF - 1, KF)
                    k_next = KD if half == 0 else k_last
                    if k_next:
                        splits(base + N_UP, N_OUT, KF, k_next)
                    else:
                        with act.Fori(0, N_OUT // 2 - 1) as i:
                            for j in range(2):
                                split(i * 2 + (base + N_UP + 2 + j), j, KF)

            splits(U_OUT_AB, N_OUT, KD, KD)
            norm(0)
            ffn(0, KD)
            norm(1)
            nc.scalar.preload_act_table_set("silu_and_others")
            with act.Fori(0, H_C) as h, step.loop(h, H_C, 0):
                base = h * N_RET + U_RET
                for i in range(N_RIN):
                    split(base + (i + 2), i % 2, KD if i < N_RIN - 2 else 4)
                    dst = rqk[:, i, :] if i < 4 else rvT[:, i - 4, :] if i < 8 else rg[:, i - 8, :]
                    nc.scalar.activation(halves(dst), bank_pair(i % 2), ACT.Copy if i < 8 else ACT.Silu)\
                        .then_inc(evicted[i % 2], 1)
                nc.scalar.preload_act_table_set("sqrt_and_others")
                for t in range(NB + 1):
                    rows = P if t < NB else 3 * TS
                    act.wait_ge(rv_done, h * (NB + 1) + (t + 1))
                    copy(rvn[0:rows, t, :], B[0:rows, 6 + t % 2, :]).then_inc(rv_ready, 1)
                act.wait_ge(rv_ready, h * (NB + 1) + (NB + 1))
                copy(vp[:, :], rvn[0:3 * TS, NB, :]).then_inc(vp_hi, 1)

                def take_output(t, bank, rows):
                    act.wait_ge(ro_done, h * (NB + 1) + (t + 1))
                    copy(onat[0:rows, t, :], B[0:rows, bank, :]).then_inc(ro_copied, 1)

                def deviation(n, first, end):
                    act.wait_ge(rvar_ready, h * 2 + (n + 1))
                    nc.scalar.activation(rrs[:, first:end], rmv[:, first:end, 1], ACT.Sqrt, bias=eps)\
                        .then_inc(rstd_ready, 1)

                def affine(et):
                    gain, shift = (tab[:, T_GN + 4 * g + et:T_GN + 4 * g + et + 1] for g in range(2))
                    act.wait_ge(rb_done, h * 5 + (et + 1))
                    nc.scalar.activation(rvT[:, et, 0:TP], B[:, et % 3, :], ACT.Identity, scale=gain, bias=shift)\
                        .then_inc(rg_taken, 1)

                for t, bank in enumerate((0, 1, 2, 6)):
                    take_output(t, bank, P)
                deviation(0, 0, NB)
                for et in range(4):
                    affine(et)
                for et in range(4):
                    if et == 3:
                        take_output(NB, 3, TS)
                        deviation(1, NB, NB + 1)
                    act.wait_ge(m_ready, h * 4 + (et + 1))
                    copy(m_hi[:, et, 0:TP], rvT[:, et, 0:TP]).then_inc(mhi_ready, 1)
                nc.scalar.preload_act_table_set("silu_and_others")
                for i in range(N_OUT):
                    split(base + (N_RIN + i + 2), i % 2, 4 if i < N_OUT - 2 else KD)
            norm(2)
            ffn(1, None)
            norm(3)

        @block.vector
        def _(dve):
            step = Count(dve, d_step)
            V = nc.vector

            def low(u, j, k):
                dve.wait_ge(hi_ready, u + 1)
                V.tensor_tensor(w_lo[:, j, 0:k * P], w_raw[:, j, 0:k * P], w_hi[:, j, 0:k * P].bitcast(F32),
                                ALU.subtract).then_inc(lo_ready, 1)

            for first, value in ((evicted[0], 1), (evicted[1], 1), (conv_done, 1), (zr_ready, 1), (o_taken, 2),
                                 (pav_done, 1), (pzr_ready, 1), (po_lo, 1), (o32_ready, 1),
                                 *((s, 16) for s in so_stored)):
                dve.sem_inc(first, value)
            low(0, 0, KD)
            for m in range(KD):
                dve.wait_ge(x_hi_ready, m + 1)
                V.tensor_tensor(x_lo[:, m, :], y[:, m, :], x_hi[:, m, :].bitcast(F32), ALU.subtract)\
                    .then_inc(x_lo_ready, 1)
            low(1, 1, KD)
            with dve.Fori(0, 4) as i:
                for j in range(2):
                    low(i * 2 + (2 + j), j, KD)

            dve.wait_ge(const_in, 5 * 16)
            dve.wait_ge(mix_in, 6 * 16)
            step.add(V.memset(vmv[:, :, :], 1.0))
            for t in range(NB + 1):
                rows = P if t < NB else TS
                dve.wait_ge(nat_b, t + 1)
                V.tensor_copy(v_nat[0:rows, t, :], B[0:rows, 6 + t % 2, :]).then_inc(cop_b, 1)
                dve.wait_ge(cop_a, t + 1)
                step.add(V.bn_stats(vst[0:rows, t, :], va_nat[0:rows, t, :]))
            step.wait()
            for t in range(NB + 1):
                rows = P if t < NB else TS
                last = V.bn_aggr(vmv[0:rows, t, :], vst[0:rows, t, :])
                if t < NB:
                    step.add(last)
            last.then_inc(va_var, 1)
            low(10, 0, KD)
            dve.wait_ge(va_std, 1)
            step.add(V.reciprocal(vrs[:, :], vrs[:, :]))
            step.wait()
            dve.wait_ge(va_var, 1)
            for t in range(NB + 1):
                rows = P if t < NB else TS
                step.add(V.tensor_scalar(va_nat[0:rows, t, :], va_nat[0:rows, t, :], vmv[0:rows, t, 0:1],
                                         vrs[0:rows, t:t + 1], ALU.subtract, ALU.mult))
            low(11, 1, KD)
            step.wait()
            for t in range(NB + 1):
                rows = P if t < NB else TS
                step.add(V.tensor_tensor(va_nat[0:rows, t, :], va_nat[0:rows, t, :], vlng[0:rows, :], ALU.mult))
            low(12, 0, KD)
            step.wait()
            for t in range(NB + 1):
                rows = P if t < NB else TS
                V.tensor_tensor(va_nat[0:rows, t, :], va_nat[0:rows, t, :], vlnb[0:rows, :], ALU.add)\
                    .then_inc(va_ready, 1)
            low(13, 1, KD)
            for g in range(8):
                step.add(V.tensor_tensor(wsT[:, g, :], wsT[:, g, :], mask_le, ALU.mult))
            w4m = cst[0:TS, 6, 80:80 + TS]
            V.tensor_tensor(w4[:, :, :], w4[:, :, :], view(w4m, (0, 8), (1, TS)), ALU.mult).then_inc(ws_ready, 1)
            low(14, 0, KD)
            step.add(V.tensor_scalar(lnp[:, :, 0, :], lnp[:, :, 0, :], -0.5, None, ALU.mult))
            step.add(V.tensor_copy(biasrow[:, :].rearrange("p (h q) -> p h q", q=4),
                                   view(bias8[:, :], (1, H_B), (0, 4))))
            step.add(V.memset(qz[:, :, :], 0.0))
            for u in range(15, 19):
                low(u, u % 2, KD)

            def dec_q(b):
                V.tensor_scalar(view(qz[:, 0, :], (40, 4), (1, 8)), view(qbd[:, 0, 0, :], (64, 4), (1, 8), off=b * 8),
                                1.0, None, ALU.mult).then_inc(qz_ready, 1)

            dve.wait_ge(zeroed, 2)
            for j in range(2):
                dve.wait_ge(evicted[j], (U_IN_AB + 16) // 2 + 1)
            for h2 in range(2):
                rows = slice(64 * h2, 64 * h2 + 64)
                V.tensor_copy(qbd[rows, :, :, 4 * h2:4 * h2 + 4],
                              qT[rows, :, TP:NT].rearrange("p c (b t) -> p c b t", t=DEC_T)).then_inc(qbd_ready, 1)
            dve.wait_ge(qbd_ready, 2)
            step.wait()
            dec_q(0)
            for u in range(19, 22):
                low(u, u % 2, KD)

            dve.wait_ge(zn_done, 1)
            for c in range(4):
                step.add(V.scalar_tensor_tensor(zn[:, c, :, :], B[0:TS, 5, c * 64:(c + 1) * 64]
                                                .rearrange("p (b h) -> p b h", h=8), 0.125,
                                                view(biasrow[0:TS, :], (0, DEC_B), (1, 8), off=c * 8),
                                                ALU.mult, ALU.add))
            step.wait()
            V.tensor_tensor(zn[:, :, :, :].rearrange("p c b h -> p c (b h)"),
                            zn[:, :, :, :].rearrange("p c b h -> p c (b h)"), view(negn, (0, 4), (1, 64)), ALU.add)\
                .then_inc(zn_ready, 1)

            def mix_gate(pr):
                dve.wait_ge(gm_mixed, pr + 2)
                if pr:
                    dve.wait_ge(gm_out, pr)
                step.add(V.tensor_tensor(gmix[:, 0:TP].rearrange("p (n t) -> p n t", t=P),
                                         B[:, pr, :].rearrange("p (n t) -> p n t", t=P),
                                         view(brep[:, pr, :], (0, NB), (1, P)), ALU.add))
                step.add(V.tensor_tensor(gmix[:, TP:NT].rearrange("p (b t) -> p b t", t=DEC_T),
                                         B[:, 6, pr * TS:(pr + 1) * TS].rearrange("p (b t) -> p b t", t=DEC_T),
                                         view(brep[:, pr, :], (0, DEC_B), (1, DEC_T)), ALU.add))
                step.wait()
                V.tensor_tensor(uT[:, pr, :], gmix[:, :], uT[:, pr, :], ALU.mult).then_inc(gm_out, 1)

            def dec_z_rows(group):
                dve.wait_ge(kv_used, group * SLOTS + SLOTS)
                V.tensor_copy(z4[:, :, :].rearrange("p a n -> p (a n)"), B[:, 4, :]).then_inc(z4_ready, 1)

            def perm(ap):
                return ap.rearrange("p (s h) -> p h s", h=32)

            def dec_z(b):
                dve.wait_ge(zt_done, b + 1)
                V.scalar_tensor_tensor(zd[:, :, :], perm(B[:, 7, :]), 0.125,
                                       view(biasrow[:, :], (1, 32), (0, 16)), ALU.mult, ALU.add).then_inc(z_ready, 1)

            for j in range(2):
                dve.wait_ge(evicted[j], N_IN_AB // 2 + 1)
            dec_z_rows(0)
            dec_q(1)
            mix_gate(0)
            mix_gate(1)
            dve.wait_ge(lnn_ready, 1)
            dve.wait_ge(zn_ready, 1)
            V.scalar_tensor_tensor(spn[0:TS, :, :, :], zn[:, :, :, :], 0.0, lnn[:, :, :, :], ALU.max, ALU.add)\
                .then_inc(spn_ready, 1)
            mix_gate(2)
            dec_z(0)
            mix_gate(3)
            dve.wait_ge(rn_done, 1)
            V.tensor_tensor(zn[:, :, :, :].rearrange("p a b c -> p (a b c)"),
                            zn[:, :, :, :].rearrange("p a b c -> p (a b c)"), B[0:TS, 5, 0:256], ALU.subtract)\
                .then_inc(znr_ready, 1)
            for pr in range(4):
                dve.wait_ge(gm_hi, pr + 1)
                V.tensor_tensor(x_lo[:, pr, :], uT[:, pr, :], x_hi[:, pr, :].bitcast(F32), ALU.subtract)\
                    .then_inc(gm_lo, 1)
            dve.wait_ge(an_ready, 1)
            dve.wait_ge(gm_lo, 4)
            dve.wait_ge(chunk_stored, 16)
            step.add(V.memset(smask[:, :, :], 1.0))
            step.wait()
            step.add(V.memset(smask[:, :, 0:1], 0.0))

            def dec_sp(b):
                dve.wait_ge(log_ready, b + 1)
                step.add(V.scalar_tensor_tensor(sp17[:, :, 1:17], zd[:, :, :], 0.0, ld[:, :, :], ALU.max, ALU.add))
                step.add(V.tensor_scalar(sp17[:, :, 0:1].rearrange("p (c h) o -> p c (h o)", c=4),
                                         view(spn[:, 0, 0, :], (64, 4), (1, 8), off=b * 8), 1.0, None, ALU.mult))
                step.wait()
                f = "p a b -> p (a b)"
                V.tensor_tensor_scan(inc17[:, :, :].rearrange(f), smask[:, :, :].rearrange(f),
                                     sp17[:, :, :].rearrange(f), 0.0, ALU.mult, ALU.add).then_inc(sp_ready, 1)

            def dec_zr(b):
                dve.wait_ge(r_done, b + 1)
                V.tensor_tensor(ad[:, :, :].rearrange("p a b -> p (a b)"), zd[:, :, :].rearrange("p a b -> p (a b)"),
                                B[:, 5, :], ALU.subtract).then_inc(zr_ready, 1)

            def dec_out(b, group):
                dve.wait_ge(kv_used, group * SLOTS + SLOTS)
                V.tensor_copy(o32[:, :], B[0:32, 6, :]).then_inc(o32_ready, 1)
                dve.wait_ge(o_done, b + 1)
                for h2 in range(2):
                    rows = slice(64 * h2, 64 * h2 + 64)
                    V.tensor_scalar(view(bsT[rows, 0, :], (TS, 4), (1, 4), off=b * 4),
                                    view(B[rows, 4, 4 * h2:4 * h2 + 4], (8, 4), (1, 4)), 1.0, None, ALU.mult)\
                        .then_inc(o_taken, 1)

            def pair_in(c):
                dve.wait_ge(pav_done, c * 2 + 1)
                for pair, whole in ((qpair, qT), (kpair, kT)):
                    V.tensor_scalar(pair[:, :], view(whole[:, 0, :], (1, TP), off=c * NT), 1.0, None, ALU.mult)\
                        .then_inc(pk_ready, 1)
                V.tensor_scalar(vpair[:, :, :], view(v_nat[:, 0, :], (512, NB), (1, P), off=c * P), 1.0, None,
                                ALU.mult).then_inc(pk_ready, 1)

            def pr_z(n):
                bias = view(bias8[:, :], (1, 1), off=n)
                dve.wait_ge(pqk_done, n + 1)
                dve.wait_ge(pav_done, n + 1)
                step.add(V.tensor_scalar(zp[:, 0:TP], B[:, 0, :], 0.125, bias, ALU.mult, ALU.add))
                step.add(V.tensor_scalar(zp[:, TP:ZW].rearrange("p (a n) -> p a n", a=2), B[:, 1:3, 0:384],
                                         0.125, bias, ALU.mult, ALU.add))
                step.wait()
                for j in range(NB):
                    last = V.tensor_tensor(zp[:, ZOFF[j]:ZOFF[j] + P], zp[:, ZOFF[j]:ZOFF[j] + P], neg_ge, ALU.add)
                    if j < NB - 1:
                        step.add(last)
                last.then_inc(pz_ready, 1)

            def pr_sp(n):
                dve.wait_ge(pz_ready, n + 1)
                dve.wait_ge(plog_ready, n + 1)
                step.add(V.scalar_tensor_tensor(lp[:, :], zp[:, :], 0.0, lp[:, :], ALU.max, ALU.add))
                step.wait()
                step.add(V.tensor_tensor(tp1[:, :], lp[:, ZOFF[2] + P:ZOFF[2] + 2 * P],
                                         lp[:, ZOFF[3]:ZOFF[3] + P], ALU.add))
                step.wait()
                V.tensor_tensor(tp0[:, 0:P], lp[:, ZOFF[1] + P:ZOFF[1] + 2 * P], lp[:, ZOFF[2]:ZOFF[2] + P],
                                ALU.add).then_inc(psp_ready, 1)
                V.tensor_tensor(tp0[:, P:2 * P], lp[:, ZOFF[1] + 2 * P:ZOFF[1] + 3 * P], tp1[:, :],
                                ALU.add).then_inc(psp_ready, 1)

            def pr_zr(n):
                dve.wait_ge(pr_done, n + 1)
                step.add(V.tensor_tensor(zp[:, 0:TP], zp[:, 0:TP], B[:, 0, :], ALU.subtract))
                V.tensor_tensor(zp[:, TP:ZW].rearrange("p (a n) -> p a n", a=2),
                                zp[:, TP:ZW].rearrange("p (a n) -> p a n", a=2), B[:, 1:3, 0:384],
                                ALU.subtract).then_inc(pzr_ready, 1)

            def pair_out(c):
                dve.wait_ge(pav_done, c * 2 + 3)
                hi = view(x_hi[:, 4, 0:TP], (1, TP), off=c * NT)
                lo = view(x_lo[:, 4, 0:TP], (1, TP), off=c * NT)
                V.tensor_scalar(hi, B[:, 3, :], 1.0, None, ALU.mult).then_inc(po_hi, 1)
                dve.wait_ge(po_hi, c + 1)
                V.tensor_tensor(lo, B[:, 3, :], hi.bitcast(F32), ALU.subtract).then_inc(po_lo, 1)

            def attend(b, last, more=True):
                dec_zr(b)
                pr_z(b)
                pr_sp(b)
                if not last:
                    dec_z_rows(b * 2 + 1)
                    if more:
                        dec_q(b + 2)
                pr_zr(b)
                if not last:
                    dve.wait_ge(zr_ready, b + 2)
                    dec_z(b + 1)
                    dve.wait_ge(z_ready, b + 2)
                    dec_sp(b + 1)
                dec_out(b, 2 * DEC_B - 1 if last else b * 2 + 2)

            pair_in(0)
            dec_sp(0)
            with dve.Fori(0, H_B // 2 - 1) as c, step.loop(c, H_B // 2 - 1, 2 * 10):
                for h2 in range(2):
                    attend(c * 2 + h2, False)
                pair_out(c)
                pair_in(c + 1)
            for h2 in range(2):
                attend(DEC_B - 2 + h2, h2 == 1, False)
            pair_out(H_B // 2 - 1)
            dve.wait_ge(bs_hi, 1)
            dve.wait_ge(o_taken, 2 * DEC_B + 2)
            V.tensor_tensor(x_lo[:, 4:8, TP:NT], bsT[:, :, :], x_hi[:, 4:8, TP:NT].bitcast(F32), ALU.subtract)\
                .then_inc(bs_lo, 1)

            def add_up(base, n_rows, residual, k, k_next, sums=False):
                def body(pair, j, kk, last=False):
                    i = pair * 2 + j
                    dve.wait_ge(tile_done, i + (base + 1))
                    out = view(y[:, 0, :], (HN, 2), (1, HN), off=i * NT)
                    V.tensor_tensor(out, out, bank_pair(j), ALU.add).then_inc(evicted[j], 1)
                    if sums:
                        step.wait()
                        dve.wait_ge(evicted[j], pair + (base // 2 + 2))
                        total = V.tensor_tensor(s1[:, :], s1[:, :], view(y[:, 0, :], (1, NT), off=i * NT), ALU.add)
                        total.then_inc(s_sum, 1) if last else step.add(total)
                    if kk:
                        low(i + (base + 2), j, kk)

                dve.wait_ge(y_scaled, residual)
                if sums:
                    step.add(V.memset(s1[:, :], 0.0))
                pairs = n_rows // 2
                with dve.Fori(0, pairs - 1) as i, step.loop(i, pairs - 1, 2 if sums else 0):
                    for j in range(2):
                        body(i, j, k)
                for j in range(2):
                    body(pairs - 1, j, k_next, j == 1)

            def norm(n):
                dve.wait_ge(m_done, n + 1)
                for m in range(KD):
                    V.tensor_tensor(halves(y[:, m, :]), halves(y[:, m, :]), B[:, 4:6, 0:HN], ALU.subtract)\
                        .then_inc(c_ready, 1)

                def scale(m):
                    V.scalar_tensor_tensor(y[:, m, :], y[:, m, :], lnp[:, n, 0, m:m + 1], std[:, :],
                                           ALU.mult, ALU.mult).then_inc(scaled, 1)

                dve.wait_ge(std_ready, n + 1)
                step.add(V.tensor_tensor(s1[:, :], std[:, :], std[:, :], ALU.mult))
                step.wait()
                step.add(V.scalar_tensor_tensor(halves(s1[:, :]), B[:, 6:8, 0:HN], eps, halves(s1[:, :]),
                                                ALU.add, ALU.mult))
                step.wait()
                step.add(V.scalar_tensor_tensor(std[:, :], s1[:, :], 3.0, std[:, :], ALU.subtract, ALU.mult))
                step.wait()
                dve.wait_ge(c_ready, (n + 1) * KD)
                scale(0)
                for m in range(KD):
                    if m < KD - 1:
                        scale(m + 1)
                    if n < 3:
                        dve.wait_ge(scaled, n * KD + m + 1)
                        dve.wait_ge(lnhi_ready, n * KD + m + 1)
                        V.scalar_tensor_tensor(x_lo[:, m, :], y[:, m, :], lnp[:, n, 1, m:m + 1],
                                               x_hi[:, m, :].bitcast(F32), ALU.add, ALU.subtract)\
                            .then_inc(ln_done, 1)

            def ffn(l, k_last):
                for half in range(2):
                    base = U_FFN[l] + half * (N_UP + N_OUT)
                    pairs = (2 * l + half) * KF
                    gs = view(gp[:, 0:1], (6, DEC_B), (1, 2), off=TP + 2)

                    def pair(i, k):
                        tile = i + half * KF
                        w = lambda t: view(cw[:, l, 0, :], (1, 1), off=tile * 4 + t)
                        low(i * 2 + (base + 2), 0, k)
                        dve.wait_ge(evicted[0], i + (base // 2 + 2))
                        step.add(V.tensor_scalar(gs, view(cstate[:, l, 0, :], (2, DEC_B), (1, 2), off=tile * 16),
                                                 1.0, None, ALU.mult))
                        step.add(V.tensor_scalar(view(cso[:, l, 0, :], (1, 2), off=tile * 18), gp[:, TP:TP + 2],
                                                 1.0, None, ALU.mult))
                        step.add(V.tensor_scalar(view(cso[:, l, 0, :], (2, DEC_B), (1, 2), off=tile * 18 + 2),
                                                 view(gp[:, 0:1], (6, DEC_B), (1, 2), off=TP + 6), 1.0, None, ALU.mult))
                        step.wait()
                        step.add(V.tensor_scalar(gc[:, :], gp[:, 0:GC], w(0), w(3), ALU.mult, ALU.add))
                        step.wait()
                        step.add(V.scalar_tensor_tensor(gc[:, :], gp[:, 1:GC + 1], w(1), gc[:, :], ALU.mult, ALU.add))
                        step.wait()
                        V.scalar_tensor_tensor(gc[:, :], gp[:, 2:GC + 2], w(2), gc[:, :], ALU.mult, ALU.add)\
                            .then_inc(conv_done, 1)
                        low(i * 2 + (base + 3), 1, k)
                        dve.wait_ge(gelu_ready, i + (pairs + 1))
                        dve.wait_ge(tile_done, i * 2 + (base + 2))
                        step.add(V.tensor_tensor(af[:, 0:HN], ge[:, 0:HN], B[:, 2, 0:HN], ALU.mult))
                        step.add(V.tensor_tensor(af[:, HN:TP], ge[:, HN:TP], B[:, 3, 0:TP - HN], ALU.mult))
                        V.tensor_tensor(af[:, TP:NT].rearrange("p (b t) -> p b t", t=DEC_T),
                                        view(ge[:, 0:1], (6, DEC_B), (1, DEC_T), off=TP + 2),
                                        B[:, 3, TP - HN:HN].rearrange("p (b t) -> p b t", t=DEC_T), ALU.mult)\
                            .then_inc(evicted[1], 1)
                        hi = view(act_hi[:, 0, :], (1, NT), off=i * NT)
                        step.wait()
                        dve.wait_ge(evicted[1], i + (base // 2 + 2))
                        step.add(V.tensor_scalar(hi, af[:, :], 1.0, None, ALU.mult))
                        step.wait()
                        V.tensor_tensor(view(act_lo[:, 0, :], (1, NT), off=i * NT), af[:, :], hi.bitcast(F32),
                                        ALU.subtract).then_inc(act_ready, 1)

                    if half == 0:
                        step.add(V.memset(gp[:, 0:2], 0.0))
                    with dve.Fori(0, KF - 1) as i, step.loop(i, KF - 1, 8):
                        pair(i, KD)
                    pair(KF - 1, KF)
                    add_up(base + N_UP, N_OUT, 1 + KD * (1 + 2 * l), KF, KD if half == 0 else k_last, half == 1)

            add_up(U_OUT_AB, N_OUT, 1, KD, KD, True)
            norm(0)
            dve.wait_ge(stored, 2 * 16)
            ffn(0, KD)
            norm(1)

            dve.wait_ge(y_scaled, 1 + 2 * KD)
            dve.wait_ge(zeroed, 3)
            step.add(V.memset(rmv[:, :, :], 1.0))
            with dve.Fori(0, H_C) as h, step.loop(h, H_C, RET_STEPS):
                base = h * N_RET + U_RET
                for i in range(N_RIN):
                    low(base + (i + 2), i % 2, KD if i < N_RIN - 2 else 4)
                dve.wait_ge(tab_in, h * 16 + 16)
                dve.wait_ge(roped, h * 4 + 4)
                for dt in range(2):
                    V.tensor_tensor(view(qm[:, dt, 0, :], (TS + DEC_T, DEC_B), (1, DEC_T)),
                                    rqk[:, dt, TP:NT].rearrange("p (b t) -> p b t", t=DEC_T),
                                    tab[:, T_QD:T_QD + TS].rearrange("p (b t) -> p b t", t=DEC_T), ALU.mult)\
                        .then_inc(qm_ready, 1)
                for t in range(NB + 1):
                    rows = P if t < NB else 3 * TS
                    dve.wait_ge(rt_done, h * (NB + 1) + (t + 1))
                    V.tensor_scalar(rkn[0:rows, t, :], B[0:rows, 4 + t % 2, 0:DK], tab[0:rows, T_KP + t:T_KP + t + 1],
                                    None, ALU.mult).then_inc(rk_ready, 1)
                dve.wait_ge(rk_ready, h * (NB + 1) + (NB + 1))
                V.tensor_scalar(kp[:, :], rkn[0:3 * TS, NB, :], 1.0, None, ALU.mult).then_inc(kp_hi, 1)
                dve.wait_ge(kp_hi, h + 1)
                V.tensor_tensor(kp[2 * TS:3 * TS, :], rkn[2 * TS:3 * TS, NB, :], kp[2 * TS:3 * TS, :].bitcast(F32),
                                ALU.subtract).then_inc(kp_ready, 1)
                for j, (bank, c0) in enumerate(((0, 0), (1, 0), (2, 0), (2, 256))):
                    dve.wait_ge(sc_done, h * 3 + min(j + 1, 3))
                    V.tensor_tensor(scT[:, ZOFF[j]:ZOFF[j] + CAUSAL[j]], B[:, bank, c0:c0 + CAUSAL[j]],
                                    tab[:, T_DEC:T_DEC + CAUSAL[j]], ALU.mult).then_inc(sc_ready, 1)
                dve.wait_ge(scs_done, h + 1)
                V.tensor_tensor(scs[:, :], B[0:TS, 3, 0:TS], tab[0:TS, T_SS:T_SS + TS], ALU.mult).then_inc(scs_ready, 1)
                dve.wait_ge(vp_hi, h + 1)
                V.tensor_tensor(vp[TS:2 * TS, :], rvn[TS:2 * TS, NB, :], vp[TS:2 * TS, :].bitcast(F32),
                                ALU.subtract).then_inc(vp_ready, 1)

                def state(n):
                    dve.wait_ge(st_done, h * (DEC_B + 1) + (n + 1))
                    banks = B[:, 4:6, :] if n % 2 == 0 else B[:, 6:8, :]
                    if n == 0:
                        dve.wait_ge(so_stored[RING], h * 16 + 16)
                        V.tensor_copy(s0[:, RING, :, :], banks).then_inc(so_ready, 1)
                    else:
                        old = s0[:, (n - 1) % RING, :, :]
                        V.scalar_tensor_tensor(old, old, tab[:, T_CD:T_CD + 1], banks, ALU.mult, ALU.add)\
                            .then_inc(so_ready, 1)

                def rows_of(t):
                    return P if t < NB else TS

                def stats(first, end):
                    for t in range(first, end):
                        dve.wait_ge(ro_copied, h * (NB + 1) + (t + 1))
                        step.add(V.bn_stats(rst[0:rows_of(t), t, :], onat[0:rows_of(t), t, :]))

                def variance(first, end):
                    step.wait()
                    apart(dve)
                    for t in range(first, end):
                        last = V.bn_aggr(rmv[0:rows_of(t), t, :], rst[0:rows_of(t), t, :])
                        last.then_inc(rvar_ready, 1) if t == end - 1 else step.add(last)

                def inverse(n, first, end):
                    dve.wait_ge(rstd_ready, h * 2 + (n + 1))
                    step.add(V.reciprocal(rrs[:, first:end], rrs[:, first:end]))
                    step.wait()
                    dve.wait_ge(rvar_ready, h * 2 + (n + 1))

                def normed(first, end):
                    for t in range(first, end):
                        rows = rows_of(t)
                        V.tensor_scalar(onat[0:rows, t, :], onat[0:rows, t, :], rmv[0:rows, t, 0:1],
                                        rrs[0:rows, t:t + 1], ALU.subtract, ALU.mult).then_inc(rnorm, 1)

                def gate(et):
                    dve.wait_ge(rg_taken, h * 4 + (et + 1))
                    V.tensor_tensor(rvT[:, et, 0:TP], rvT[:, et, 0:TP], rg[:, et, 0:TP], ALU.mult).then_inc(m_ready, 1)

                def gate_low(et):
                    dve.wait_ge(mhi_ready, h * 4 + (et + 1))
                    dve.wait_ge(m_ready, h * 4 + (et + 1))
                    V.tensor_tensor(m_lo[:, et, 0:TP], rvT[:, et, 0:TP], m_hi[:, et, 0:TP].bitcast(F32), ALU.subtract)\
                        .then_inc(mlo_ready, 1)

                def gate_samples():
                    ms, gs = rvT[:, :, TP:NT], rg[:, :, TP:NT]
                    dve.wait_ge(rb_done, h * 5 + 5)
                    step.add(V.tensor_tensor(ms, B[:, 3, 0:4 * TS].rearrange("p (a t) -> p a t", a=4),
                                             view(tab[:, T_GN:T_GN + 1], (1, 4), (0, TS)), ALU.mult))
                    step.wait()
                    step.add(V.tensor_tensor(ms, ms, view(tab[:, T_GN:T_GN + 1], (1, 4), (0, TS), off=4), ALU.add))
                    step.wait()
                    step.add(V.tensor_tensor(ms, ms, gs, ALU.mult))
                    step.wait()
                    step.add(V.tensor_scalar(m_hi[:, :, TP:NT], ms, 1.0, None, ALU.mult))
                    step.wait()
                    V.tensor_tensor(m_lo[:, :, TP:NT], ms, m_hi[:, :, TP:NT].bitcast(F32), ALU.subtract)\
                        .then_inc(mlo_ready, 1)

                state(0)
                stats(0, NB)
                variance(0, NB)
                inverse(0, 0, NB)
                normed(0, NB)
                state(1)
                state(2)
                state(3)
                gate(0)
                state(4)
                gate(1)
                gate(2)
                state(5)
                gate(3)
                gate_low(0)
                state(6)
                stats(NB, NB + 1)
                variance(NB, NB + 1)
                gate_low(1)
                inverse(1, NB, NB + 1)
                normed(NB, NB + 1)
                gate_low(2)
                gate_low(3)
                gate_samples()
                state(7)
                state(8)
                step.add(V.memset(s1[:, :], 0.0))
                for i in range(N_OUT):
                    dve.wait_ge(tile_done, base + (N_RIN + i + 1))
                    V.tensor_tensor(halves(y[:, i, :]), halves(y[:, i, :]), bank_pair(i % 2), ALU.add)\
                        .then_inc(evicted[i % 2], 1)
                    step.wait()
                    dve.wait_ge(evicted[i % 2], h * (N_RET // 2) + (i // 2 + (U_RET + N_RIN) // 2 + 2))
                    step.add(V.tensor_tensor(s1[:, :], s1[:, :], y[:, i, :], ALU.add))
                    low(base + (N_RIN + i + 2), i % 2, 4 if i < N_OUT - 2 else KD)
            step.wait()
            dve.sem_inc(s_sum, 1)
            norm(2)
            ffn(1, None)
            norm(3)

        @block.tensor
        def _(pe):
            mm = nc.tensor.matmul

            def product(base, n, k, hi, lo, k_ready):
                with pe.Fori(0, n // 2) as i:
                    for j in range(2):
                        pe.wait_ge(lo_ready, i * 2 + (base + j + 1))
                        pe.wait_ge(evicted[j], i + (base // 2 + 1))
                        tile_body(j, k, hi, lo, k_ready if j == 0 else None)

            def tile_body(j, k, hi, lo, k_ready=None):
                for kt in range(k):
                    if k_ready:
                        k_ready(kt)
                    w = slice(kt * P, (kt + 1) * P)
                    for n, (a, x) in enumerate(((w_hi, hi), (w_hi, lo), (w_lo, hi))):
                        for half in range(2):
                            last = mm(B[:, 2 * j + half, 0:HN], a[:, j, w], x[:, kt, half * HN:(half + 1) * HN],
                                      start=kt == 0 and n == 0, stop=kt == k - 1 and n == 2)
                last.then_inc(tile_done, 1)

            product(U_IN_AB, 8, KD, x_hi, x_lo, lambda kt: pe.wait_ge(x_lo_ready, kt + 1))

            pe.wait_ge(const_in, 5 * 16)
            for j in range(2):
                pe.wait_ge(evicted[j], (U_IN_AB + 8) // 2 + 1)
            for t in range(NB + 1):
                rows = P if t < NB else TS
                for first, bank, taken, done in ((0, 4, cop_a, nat_a), (4, 6, cop_b, nat_b)):
                    if t >= 2:
                        pe.wait_ge(taken, t - 1)
                    for f in range(4):
                        last = nc.tensor.transpose(B[0:rows, bank + t % 2, f * P:(f + 1) * P],
                                                   y[:, first + f, t * P:t * P + rows], ident)
                    last.then_inc(done, 1)
            product(U_IN_AB + 8, N_IN_AB - 8, KD, x_hi, x_lo, None)

            for j in range(2):
                pe.wait_ge(evicted[j], N_IN_AB // 2 + 1)
            pe.wait_ge(qbd_ready, 2)
            pe.wait_ge(cop_a, NB + 1)
            pe.wait_ge(cop_b, NB + 1)
            for c in range(4):
                last = mm(B[0:TS, 5, c * 64:(c + 1) * 64], kT[:, c, TP:NT],
                          qbd[:, c, :, :].rearrange("p b h -> p (b h)"), start=True, stop=True)
            last.then_inc(zn_done, 1)

            def of_b(t, c, b):
                return view(t[:, c, 0, :], (1, 8), off=b * 8)

            def qk(b, group, slots=range(SLOTS)):
                for s in slots:
                    pe.wait_ge(kv_landed[s], group * 32 + 32)
                    for g in range(PER_SLOT):
                        k, r = divmod(PER_SLOT * s + g, 4)
                        for c in range(4):
                            last = mm(B[32 * r:32 * r + 32, 4, k * P:(k + 1) * P], qz[:, c, :],
                                      kv[:, s, g, c * P:(c + 1) * P], start=c == 0, stop=c == 3)
                    last.then_inc(kv_used, 1)

            def z_columns(b):
                pe.wait_ge(z4_ready, b + 1)
                if not isinstance(b, int) or b:
                    pe.wait_ge(z_ready, b)
                for k in range(4):
                    last = nc.tensor.transpose(B[:, 7, k * P:(k + 1) * P], z4[:, k, :], ident)
                last.then_inc(zt_done, 1)

            def suffix(b):
                pe.wait_ge(sp_ready, b + 1)
                pe.wait_ge(zr_ready, b + 1)
                mm(B[:, 5, :], tri, sp17[:, :, 1:17], start=True, stop=False)
                mm(B[:, 5, :], ones, inc17[:, :, 0:16], start=False, stop=True).then_inc(r_done, 1)

            def av(b, group, slots):
                if slots[0] == 0:
                    pe.wait_ge(a_ready, b + 1)
                    pe.wait_ge(o32_ready, b + 1)
                for s in slots:
                    pe.wait_ge(kv_landed[s], group * 32 + 32)
                    for g in range(PER_SLOT):
                        page = PER_SLOT * s + g
                        last = mm(B[0:32, 6, :], ad[:, :, page], kv[:, s, g, :], start=page == 0,
                                  stop=page == N_PAGES - 1)
                    last.then_inc(kv_used, 1)

            def av_columns(b):
                pe.wait_ge(o32_ready, b + 2)
                for c in range(4):
                    mm(B[:, 4, c * 8:(c + 1) * 8], v_nat[0:TS, NB, c * P:(c + 1) * P], of_b(an, c, b),
                       start=True, stop=False)
                    last = mm(B[:, 4, c * 8:(c + 1) * 8], o32[:, c * P:(c + 1) * P],
                              ident[0:32, c * 8:(c + 1) * 8], start=False, stop=True)
                last.then_inc(o_done, 1)

            def zbank(j, c0, w):
                c0 += 256 if j == 3 else 0
                return B[:, min(j, 2), c0:c0 + w]

            def pr_qk(n, h2):
                rows = slice(64 * h2, 64 * h2 + 64)
                pe.wait_ge(pzr_ready, n + 1)
                for j in range(NB):
                    last = mm(zbank(j, 0, CAUSAL[j]), kpair[rows, j * P:(j + 1) * P],
                              qpair[rows, j * P:TP], start=True, stop=True)
                last.then_inc(pqk_done, 1)

            def pr_suffix(n):
                pe.wait_ge(psp_ready, n * 2 + 2)
                for j, behind in ((0, ((1, lp[:, ZOFF[1]:ZOFF[1] + P]), (2, tp0[:, :]))),
                                  (1, ((1, lp[:, ZOFF[2]:ZOFF[2] + P]), (2, tp1[:, :]))),
                                  (2, ((1, lp[:, ZOFF[3]:ZOFF[3] + P]),)), (3, ())):
                    last = mm(zbank(j, 0, CAUSAL[j]), tri, lp[:, ZOFF[j]:ZOFF[j] + CAUSAL[j]], start=True,
                              stop=not behind)
                    for i, (blk, t) in enumerate(behind):
                        last = mm(zbank(j, blk * P, t.shape[1]), ones, t, start=False, stop=i == len(behind) - 1)
                last.then_inc(pr_done, 1)

            def pr_av(n, h2):
                rows = slice(64 * h2, 64 * h2 + 64)
                pe.wait_ge(pa_ready, n + 1)
                for j in range(NB):
                    last = mm(B[rows, 3, j * P:TP], vpair[:, j, 64 * h2:64 * h2 + 64],
                              zp[:, ZOFF[j]:ZOFF[j] + CAUSAL[j]], start=j == 0, stop=j == NB - 1)
                last.then_inc(pav_done, 1)

            def attend(c, h2, last):
                b = c * 2 + h2
                suffix(b)
                if not last:
                    pe.wait_ge(qz_ready, b + 2)
                    pe.wait_ge(o_taken, b * 2 + 2)
                    qk(b + 1, b * 2 + 1, range(2))
                if h2 == 0:
                    pe.wait_ge(pk_ready, c * 3 + 3)
                pr_qk(b, h2)
                if not last:
                    qk(b + 1, b * 2 + 1, range(2, SLOTS))
                group = 2 * DEC_B - 1 if last else b * 2 + 2
                av(b, group, range(SLOTS // 2))
                pr_suffix(b)
                if not last:
                    z_columns(b + 1)
                av(b, group, range(SLOTS // 2, SLOTS))
                if h2 == 0:
                    pe.wait_ge(po_lo, c + 1)
                pr_av(b, h2)
                av_columns(b)

            pe.wait_ge(qz_ready, 1)
            qk(0, 0)

            pe.wait_ge(ws_ready, 1)
            pe.wait_ge(va_ready, NB + 1)
            for g in range(8):
                last = mm(B[64 * (g % 2):64 * (g % 2) + 64, 6, (g // 2) * TS:(g // 2 + 1) * TS],
                          va_nat[0:TS, NB, g * 64:(g + 1) * 64], w4[:, g, :], start=True, stop=True)
            last.then_inc(gm_mixed, 1)
            for pr in range(4):
                for g2 in range(2):
                    g = 2 * pr + g2
                    for n in range(NB):
                        last = mm(B[64 * g2:64 * g2 + 64, pr, n * P:(n + 1) * P], va_nat[:, n, g * 64:(g + 1) * 64],
                                  wsT[:, g, :], start=True, stop=True)
                last.then_inc(gm_mixed, 1)
                if pr == 1:
                    z_columns(0)
            pe.wait_ge(spn_ready, 1)
            mm(B[0:TS, 5, 0:256], tri[0:TS, 0:TS], spn[0:TS, :, :, :].rearrange("p a b c -> p (a b c)"),
               start=True, stop=True).then_inc(rn_done, 1)
            pe.wait_ge(gm_out, 4)
            pe.wait_ge(an_ready, 1)

            def attend_pair(c, last):
                for h2 in range(2):
                    attend(c, h2, last and h2 == 1)

            with pe.Fori(0, H_B // 2 - 1) as c:
                attend_pair(c, False)
            attend_pair(H_B // 2 - 1, True)

            def norm(n):
                pe.wait_ge(s_sum, n + 1)
                for half in range(2):
                    last = mm(B[:, 4 + half, 0:HN], mean_mat, s1[:, half * HN:(half + 1) * HN], start=True, stop=True)
                last.then_inc(m_done, 1)
                for m in range(KD):
                    pe.wait_ge(sq_ready, n * KD + m + 1)
                    for half in range(2):
                        last = mm(B[:, 6 + half, 0:HN], mean_mat, sq[:, m % 2, half * HN:(half + 1) * HN],
                                  start=m == 0, stop=m == KD - 1)
                    last.then_inc(sq_used, 1)

            def ffn(l):
                for half in range(2):
                    base = U_FFN[l] + half * (N_UP + N_OUT)
                    product(base, N_UP, KD, x_hi, x_lo, lambda kt: pe.wait_ge(ln_done, 2 * l * KD + kt + 1))
                    product(base + N_UP, N_OUT, KF, act_hi, act_lo,
                            lambda kt: pe.wait_ge(act_ready, (2 * l + half) * KF + kt + 1))

            def mixed(kt):
                if kt < 4:
                    pe.wait_ge(gm_lo, kt + 1)
                else:
                    pe.wait_ge(bs_lo, 1)
                    pe.wait_ge(po_lo, kt - 4 + 2)

            product(U_OUT_AB, N_OUT, KD, x_hi, x_lo, mixed)
            norm(0)
            ffn(0)
            norm(1)
            with pe.Fori(0, H_C) as h:
                with pe.Fori(0, N_RIN // 2) as i:
                    for j in range(2):
                        pe.wait_ge(lo_ready, h * N_RET + (i * 2 + (U_RET + j + 1)))
                        pe.wait_ge(evicted[j], h * (N_RET // 2) + (i + U_RET // 2 + 1))
                        tile_body(j, KD, x_hi, x_lo,
                                  (lambda kt: pe.wait_ge(ln_done, KD + kt + 1)) if j == 0 else None)
                pe.wait_ge(roped, h * 4 + 4)
                for j in range(2):
                    pe.wait_ge(evicted[j], h * (N_RET // 2) + (U_RET // 2 + N_RIN // 2 + 1))
                def rows_to(out, features):
                    return mm(out, features, ident, start=True, stop=True)

                for t in range(NB + 1):
                    rows, spots = (P, (0,)) if t < NB else (TS, (0, TS, 2 * TS))
                    if t >= 2:
                        pe.wait_ge(rk_ready, h * (NB + 1) + (t - 1))
                    for p0 in spots:
                        for f in range(2):
                            to = B[p0:p0 + rows, 4 + t % 2, f * P:(f + 1) * P]
                            last = (nc.tensor.transpose(to, rqk[:, 2 + f, t * P:t * P + rows], ident) if t < NB
                                    else rows_to(to, rqk[:, 2 + f, TP:NT]))
                    last.then_inc(rt_done, 1)
                    if t >= 2:
                        pe.wait_ge(rv_ready, h * (NB + 1) + (t - 1))
                    for p0 in spots:
                        for f in range(4):
                            to = B[p0:p0 + rows, 6 + t % 2, f * P:(f + 1) * P]
                            last = (nc.tensor.transpose(to, rvT[:, f, t * P:t * P + rows], ident) if t < NB
                                    else rows_to(to, rvT[:, f, TP:NT]))
                    last.then_inc(rv_done, 1)
                for j in range(NB):
                    for dt in range(2):
                        last = mm(zbank(j, 0, CAUSAL[j]), rqk[:, 2 + dt, j * P:(j + 1) * P], rqk[:, dt, j * P:TP],
                                  start=dt == 0, stop=dt == 1)
                    if j != 2:
                        last.then_inc(sc_done, 1)
                for dt in range(2):
                    last = mm(B[0:TS, 3, 0:TS], rqk[:, 2 + dt, TP:NT], rqk[:, dt, TP:NT], start=dt == 0, stop=dt == 1)
                last.then_inc(scs_done, 1)
                pe.wait_ge(rk_ready, h * (NB + 1) + (NB + 1))
                pe.wait_ge(rv_ready, h * (NB + 1) + (NB + 1))
                for dt in range(2):
                    for j in range(NB):
                        last = mm(B[:, 4 + dt, :], rkn[:, j, dt * P:(dt + 1) * P], rvn[:, j, :],
                                  start=j == 0, stop=j == NB - 1)
                last.then_inc(st_done, 1)
                pe.wait_ge(sc_ready, h * 4 + 4)
                for t, bank in enumerate((0, 1, 2, 6)):
                    for j in range(t + 1):
                        c0 = ZOFF[j] + (t - j) * P
                        last = mm(B[:, bank, :], scT[:, c0:c0 + P], rvn[:, j, :], start=j == 0, stop=j == t)
                    last.then_inc(ro_done, 1)

                def sample_output(b):
                    pe.wait_ge(s0_landed[b % RING], h * (16 * uses(b % RING)) + 16 * (b // RING + 1))
                    for dt in range(2):
                        last = mm(B[0:TS, 3, :], qm[:, dt, b, :], s0[:, b % RING, dt, :], start=False,
                                  stop=b == DEC_B - 1 and dt == 1)
                    if b == DEC_B - 1:
                        last.then_inc(ro_done, 1)

                def sample_state(b):
                    pe.wait_ge(km_ready, h * DEC_B + (b + 1))
                    if b == 0:
                        pe.wait_ge(vp_ready, h + 1)
                        pe.wait_ge(ro_copied, h * (NB + 1) + NB)
                    else:
                        pe.wait_ge(so_ready, h * (DEC_B + 1) + b)
                    for dt in range(2):
                        last = mm(B[:, (6 if b % 2 == 0 else 4) + dt, :], km[:, b % 2, dt * P:(dt + 1) * P],
                                  vp[:, :], start=True, stop=True)
                    last.then_inc(st_done, 1)

                def back(et):
                    for t in range(NB):
                        if et == 0:
                            pe.wait_ge(rnorm, h * 5 + (t + 1))
                        last = nc.tensor.transpose(B[:, et % 3, t * P:(t + 1) * P],
                                                   onat[:, t, et * P:(et + 1) * P], ident)
                    last.then_inc(rb_done, 1)

                pe.wait_ge(scs_ready, h + 1)
                pe.wait_ge(qm_ready, h * 2 + 2)
                apart(pe)
                mm(B[0:TS, 3, :], scs[:, :], rvn[0:TS, NB, :], start=True, stop=False)
                sample_output(0)
                sample_output(1)
                for b in range(DEC_B):
                    if b + 2 < DEC_B:
                        sample_output(b + 2)
                    sample_state(b)
                    if b == 1:
                        for et in range(3):
                            back(et)
                    if b == 2:
                        pe.wait_ge(rg_taken, h * 4 + 1)
                        back(3)
                    if b == 7:
                        pe.wait_ge(rnorm, h * 5 + 5)
                        apart(pe)
                        for et in range(4):
                            last = nc.tensor.transpose(B[:, 3, et * TS:(et + 1) * TS],
                                                       onat[0:TS, NB, et * P:(et + 1) * P], ident[0:TS, 0:TS])
                        last.then_inc(rb_done, 1)
                pe.wait_ge(mlo_ready, h * 5 + 5)
                apart(pe)
                with pe.Fori(0, N_OUT // 2) as i:
                    for j in range(2):
                        pe.wait_ge(lo_ready, h * N_RET + (i * 2 + (U_RET + N_RIN + j + 1)))
                        pe.wait_ge(evicted[j], h * (N_RET // 2) + (i + (U_RET + N_RIN) // 2 + 1))
                        tile_body(j, 4, m_hi, m_lo)
            norm(2)
            ffn(1)
            norm(3)


RET_STEPS = 14 + 9


def decays(h):
    return np.log1p(-(2.0 ** (-5.0 - h)))


def constants():
    i = np.arange(P)
    cst = np.zeros((P, 7, P), np.float32)
    cst[:, 0] = np.eye(P)
    cst[:, 1] = 1.0
    cst[:, 2] = i[:, None] >= i[None, :]
    cst[:, 3] = i[:, None] <= i[None, :]
    cst[:, 4] = np.where(i[:, None] >= i[None, :], MASKED, 0.0)
    cst[:, 5] = 1.0 / D
    r = np.arange(TS)
    col = np.arange(64)
    ok = (r[:, None] // DEC_T == col[None, :] // 8) & (r[:, None] % DEC_T < col[None, :] % DEC_T)
    cst[:TS, 6, 0:64] = np.where(ok, 0.0, MASKED)
    cst[:3 * TS, 6, 64:72] = np.tile(r[:, None] // DEC_T == np.arange(DEC_B)[None, :], (3, 1))
    cst[:, 6, 72] = EPS
    same = r[:, None] // DEC_T == r[None, :] // DEC_T
    cst[:TS, 6, 80:80 + TS] = same & (r[:, None] <= r[None, :])

    pos = np.concatenate([np.arange(TP), np.tile(PAST + np.arange(DEC_T), DEC_B)]).astype(np.float32)
    inv = np.float32(10000.0) ** (-np.arange(P, dtype=np.float32) / np.float32(P))
    ang = inv[:, None].astype(np.float32) * pos[None, :]
    rope = np.stack([np.cos(ang), np.sin(ang)], 1).astype(np.float32)

    tab = np.zeros((H_C, P, T_W), np.float64)
    for h in range(H_C):
        g = decays(h)
        d = np.arange(TP)[None, :] - i[:, None]
        tab[h, :, T_DEC:T_DEC + TP] = np.where(d >= 0, np.exp(d * g), 0.0) / 16.0
        for j in range(NB):
            tab[h, :, T_KP + j] = np.exp((TP - 1 - (j * P + i)) * g) / 16.0
        tab[h, :3 * TS, T_KS] = np.tile(np.exp((DEC_T - 1 - r % DEC_T) * g) / 16.0, 3)
        tab[h, :, T_QD:T_QD + TS] = np.exp((r % DEC_T + 1) * g)[None, :]
        dd = r[None, :] - r[:, None]
        tab[h, :TS, T_SS:T_SS + TS] = np.where(same & (dd >= 0), np.exp(dd * g), 0.0) / 16.0
        tab[h, :, T_CD] = np.exp(DEC_T * g)
    return cst, rope, tab.astype(np.float32)


def lay_out(x_prompt, x_sample, cache_sb_k, cache_sb_v, state_ret, state_ffn_conv, page_table,
            w_in_ab, vln_g, vln_b, w_s, b_s, sb_bias, w_out_ab, w_in_ret, gn_g, gn_b, w_out_ret,
            ln1_g, ln1_b, ln2_g, ln2_b, w_up, conv_w, conv_b, w_down):
    C = np.ascontiguousarray

    def pack(w, order=None):
        k, m = w.shape
        t = w.reshape(k // P, P, m // P, P).transpose(2, 1, 0, 3).reshape(m // P, P, k)
        return C(t if order is None else t[order])

    cst, rope, tab = constants()
    rows = lambda x: x.reshape(-1, P).T
    gn = np.stack([gn_g[0].reshape(H_C, 4, P), gn_b[0].reshape(H_C, 4, P)], 1)
    tab[:, :, T_GN:T_GN + 8] = gn.transpose(0, 3, 1, 2).reshape(H_C, P, 8)
    xs = np.concatenate([x_prompt[0], x_sample.reshape(TS, D)], 0)
    out = {"xT": C(xs.T.reshape(KD, P, NT).transpose(1, 0, 2)), "cst": cst, "rope": rope, "tab": tab}
    out["w_in_ab"] = pack(w_in_ab[0], [4, 5, 6, 7, 16, 17, 18, 19, 0, 1, 2, 3, 8, 9, 10, 11, 12, 13, 14, 15])
    out["w_out_ab"] = pack(w_out_ab[0])
    gv = [n for t in range(NFF) for n in (t, NFF + t)]
    out["w_up"] = np.concatenate([pack(w_up[l], gv) for l in range(LAYERS)])
    out["w_dn"] = C(w_down.reshape(LAYERS, 2, KF, P, KD, P).transpose(0, 1, 4, 3, 2, 5)
                    .reshape(LAYERS * 2 * KD, P, KF * P))
    out["w_rin"] = pack(w_in_ret[0], [n for h in range(H_C) for n in (
        2 * h, 2 * h + 1, 8 + 2 * h, 9 + 2 * h, *range(16 + 4 * h, 20 + 4 * h), *range(32 + 4 * h, 36 + 4 * h))])
    out["w_rout"] = C(w_out_ret[0].reshape(H_C, 4, P, KD, P).transpose(0, 3, 2, 1, 4).reshape(H_C * KD, P, 4 * P))
    pool = cache_sb_k.shape[1]
    out["kc"] = C(cache_sb_k[0].reshape(pool, P, 4, P).transpose(0, 3, 2, 1).reshape(pool, P, 512))
    out["vc"] = C(cache_sb_v[0].reshape(pool, P, 512))
    out["ptab"] = C(page_table[:, ::-1].reshape(1, DEC_B * N_PAGES))
    out["vlng"] = C(np.broadcast_to(vln_g[0], (P, 512)))
    out["vlnb"] = C(np.broadcast_to(vln_b[0], (P, 512)))
    out["bias8"] = C(np.broadcast_to(sb_bias[0], (P, H_B)))
    out["wsT"] = C(w_s[0].transpose(2, 0, 1))
    out["w4"] = C(np.tile(w_s[0, :, :DEC_T, :DEC_T].transpose(2, 0, 1), (DEC_B, 1, DEC_B)))
    out["brep"] = C(np.repeat(b_s[0].reshape(4, 2, P).transpose(1, 0, 2), 64, 0))
    ln = np.stack([np.stack([ln1_g, ln1_b], 1), np.stack([ln2_g, ln2_b], 1)], 1).reshape(4, 2, KD, P)
    out["lnp"] = C(ln.transpose(3, 0, 1, 2))
    cwb = np.concatenate([conv_w, conv_b[:, None]], 1).reshape(LAYERS, 4, NFF, P)
    out["cw"] = C(cwb.transpose(3, 0, 2, 1))
    out["cstate"] = C(state_ffn_conv.reshape(LAYERS, 2 * DEC_B, NFF, P).transpose(3, 0, 2, 1))
    out["s0"] = C(state_ret[0].reshape(DEC_B, H_C, 2, P, DV).transpose(1, 0, 3, 2, 4)
                  .reshape(H_C * DEC_B, P, 2 * DV))
    return out


OUTS = {"yT": (P, KD, NT), "kT": (P, 4, NT), "vT": (P, 4, NT), "chunk_v": (TS, 512),
        "ret_p": (H_C, P, 2 * DV), "ret_s": (H_C * DEC_B, P, 2 * DV), "conv_out": (LAYERS, P, NFF * 18)}


def give_back(o):
    C = np.ascontiguousarray
    yt = o["yT"].transpose(2, 1, 0).reshape(NT, D)
    kt = o["kT"].transpose(2, 1, 0).reshape(NT, 512)
    vt = o["vT"].transpose(2, 1, 0).reshape(NT, 512)
    cv = o["conv_out"].reshape(LAYERS, P, NFF, 18)
    conv_p = cv[..., 0:2].transpose(0, 3, 2, 1).reshape(LAYERS, 1, 2, DFF)
    conv_s = cv[..., 2:].reshape(LAYERS, P, NFF, DEC_B, 2).transpose(0, 3, 4, 2, 1).reshape(LAYERS, DEC_B, 2, DFF)
    rp = o["ret_p"].reshape(1, 1, H_C, P, 2, DV).transpose(0, 1, 2, 4, 3, 5).reshape(1, 1, H_C, DK, DV)
    rs = o["ret_s"].reshape(H_C, DEC_B, P, 2, DV).transpose(1, 0, 3, 2, 4).reshape(1, DEC_B, H_C, DK, DV)
    return tuple(C(a) for a in (
        yt[:TP].reshape(1, TP, D), yt[TP:].reshape(DEC_B, DEC_T, D),
        kt[:TP].reshape(1, 1, NB, P, H_B, DH_B), vt[:TP].reshape(1, 1, NB, P, H_B, DH_B),
        kt[TP:].reshape(1, DEC_B, DEC_T, H_B, DH_B), vt[TP:].reshape(1, DEC_B, DEC_T, H_B, DH_B),
        o["chunk_v"].reshape(1, DEC_B, DEC_T, 8, 64), rp, rs, conv_p, conv_s))


def kernel(**inputs):
    import concourse.bacc as bacc
    from concourse.bass_utils import run_bass_kernel_spmd

    arrays = lay_out(**{k: np.asarray(v) for k, v in inputs.items()})
    nc = bacc.Bacc("TRN2", target_bir_lowering=False, num_devices=1)
    A = {n: nc.dram_tensor("in_" + n, a.shape, mybir.dt.from_np(a.dtype), kind="ExternalInput").ap()
         for n, a in arrays.items()}
    for n, shape in OUTS.items():
        A[n] = nc.dram_tensor("out_" + n, shape, F32, kind="ExternalOutput").ap()
    build_program(nc, A)
    r = run_bass_kernel_spmd(nc, [{"in_" + n: a for n, a in arrays.items()}], core_ids=[0])
    return give_back({n: r.results[0]["out_" + n] for n in OUTS})
```
